# Optimizing a Trainium2 kernel written in Bass

```python
import jax
import jax.numpy as jnp
from jax import lax
import numpy as np

'''
Hybrid diffusion / flow-matching backbone, one inference step for two request groups
that share the same parameter arrays.

Trunk of DEPTH interleaved layers; layer i uses token mixer (i mod 3):
  0: bidirectional mLSTM matrix memory (chunkwise-parallel, exponential input gate,
     sigmoid forget gate, running-max stabiliser), one scan per direction
  1: windowed grouped-query attention (+-128 tokens) with a learned per-head sink logit,
     2-D axial rotary on latent tokens, banded 128-query blocks
  2: 2-D neighbourhood attention over the latent grid (min(8,ROWS) x 16 clamped window),
     key/value row bands gathered per query grid row, learned 2-D relative-position bias
Every layer: pre-RMSNorm + adaLN modulation (shift/scale/gate from SiLU(cond) through a
per-layer linear map) around the token mixer and around a ConvFFN (gated MLP with a
centred depthwise conv of width 3 between up-projection and activation); plain residual
adds; one final RMSNorm. Context tokens use the learned vector c_ctx as condition and read
only context tokens; latent tokens read all context tokens plus their latent neighbours.

Inputs:
  x_prompt (BATCH, SEQ, D_MODEL), x_sample (DEC_BATCH, DEC_SEQ, D_MODEL)
  state_mlstm_C (DEC_BATCH, N_A, 2, ML_HEADS, ML_DK, ML_DV)  final context mLSTM memory per dir
  state_mlstm_n (DEC_BATCH, N_A, 2, ML_HEADS, ML_DK)         final context normaliser per dir
  state_mlstm_m (DEC_BATCH, N_A, 2, ML_HEADS)                final context stabiliser per dir
  cache_swa_k / cache_swa_v (DEC_BATCH, N_B, SWA_KV, PAST_LEN, HEAD_DIM)
  cache_na_k / cache_na_v (DEC_BATCH, N_C, NA_HEADS, PAST_LEN, HEAD_DIM)
  c (DEC_BATCH, D_MODEL), c_ctx (D_MODEL,), then weights.
Outputs (tuple):
  y_prompt (BATCH, SEQ, D_MODEL)
  y_sample (DEC_BATCH, DEC_SEQ, D_MODEL)
  new_state_mlstm_C (BATCH, N_A, 2, ML_HEADS, ML_DK, ML_DV)
  new_state_mlstm_n (BATCH, N_A, 2, ML_HEADS, ML_DK)
  new_state_mlstm_m (BATCH, N_A, 2, ML_HEADS)
  new_cache_swa_k, new_cache_swa_v (BATCH, N_B, SWA_KV, SEQ, HEAD_DIM)
  new_cache_na_k, new_cache_na_v (BATCH, N_C, NA_HEADS, SEQ, HEAD_DIM)
'''

D_MODEL = 1024
BATCH = 1
SEQ = 128
DEPTH = 4
DEC_BATCH = 1
DEC_SEQ = 128
PAST_LEN = 128

GRID_W = 64
N_MIXERS = 3
N_A = (DEPTH + 2) // 3
N_B = (DEPTH + 1) // 3
N_C = DEPTH // 3
NORM_EPS = 1e-6
D_FF = 256 * ((8 * D_MODEL // 3 + 255) // 256)
FFN_CONV = 3
ML_D_IN = 2 * D_MODEL
ML_HEADS = 4
ML_DK = ML_D_IN // (2 * ML_HEADS)
ML_DV = ML_D_IN // ML_HEADS
ML_CONV = 3
ML_CHUNK = 128
HEAD_DIM = 64
SWA_HEADS = D_MODEL // HEAD_DIM
SWA_KV = SWA_HEADS // 4
SWA_WINDOW = 128
Q_BLOCK = 128
ROPE_BASE = 10000.0
NA_HEADS = D_MODEL // HEAD_DIM
NA_KH = 8
NA_KW = 16
NEG_INF = -1e30

kernel_name = 'hybrid_mlstm_swa_natten_diffusion_step'

def _rmsnorm(x, w):
    xf = x.astype(jnp.float32)
    y = xf * lax.rsqrt(jnp.mean(xf * xf, axis=-1, keepdims=True) + NORM_EPS)
    return (y * w.astype(jnp.float32)).astype(x.dtype)

def _dwconv(x, w, b):
    K, C = w.shape
    y = lax.conv_general_dilated(x, w[:, None, :].astype(x.dtype), window_strides=(1,),
                                 padding=[(K // 2, K // 2)],
                                 dimension_numbers=('NWC', 'WIO', 'NWC'),
                                 feature_group_count=C)
    return y + b.astype(x.dtype)

def _heads(x, n):
    B, T, _ = x.shape
    return x.reshape(B, T, n, -1).transpose(0, 2, 1, 3)

def _unheads(x):
    B, n, T, hd = x.shape
    return x.transpose(0, 2, 1, 3).reshape(B, T, n * hd)

def _split_qkv(h, w, n_q, n_kv):
    qkv = h @ w
    a, b = n_q * HEAD_DIM, (n_q + n_kv) * HEAD_DIM
    return _heads(qkv[..., :a], n_q), _heads(qkv[..., a:b], n_kv), _heads(qkv[..., b:], n_kv)

def _axial_rope(x):
    T, hd = x.shape[2], x.shape[3]
    half = hd // 2
    quarter = half // 2
    pos = jnp.arange(T)
    row = (pos // GRID_W).astype(jnp.float32)
    col = (pos % GRID_W).astype(jnp.float32)
    inv = jnp.power(ROPE_BASE, -jnp.arange(quarter, dtype=jnp.float32) / quarter)

    def rot(xs, p):
        ang = p[:, None] * inv[None, :]
        cos, sin = jnp.cos(ang), jnp.sin(ang)
        x1 = xs[..., :quarter].astype(jnp.float32)
        x2 = xs[..., quarter:].astype(jnp.float32)
        return jnp.concatenate([x1 * cos - x2 * sin, x2 * cos + x1 * sin], axis=-1)

    return jnp.concatenate([rot(x[..., :half], row), rot(x[..., half:], col)], axis=-1).astype(x.dtype)

def _q_blocks(q, n_kv, bs):
    B, H, T, hd = q.shape
    return jnp.moveaxis(q.reshape(B, n_kv, H // n_kv, T // bs, bs, hd), 3, 0)

def _merge_blocks(o):
    nb, B, KV, G, bs, hd = o.shape
    return jnp.moveaxis(o, 0, 3).reshape(B, KV * G, nb * bs, hd)

def _attend(q, parts, sink):
    scale = q.shape[-1] ** -0.5
    logits = []
    for k_, v_, bias in parts:
        s = jnp.einsum('bkgqd,bksd->bkgqs', q, k_).astype(jnp.float32) * scale
        if bias is not None:
            s = s + bias
        logits.append(s)
    if sink is not None:
        logits.append(jnp.broadcast_to(sink.astype(jnp.float32)[None, :, :, None, None],
                                       logits[0].shape[:-1] + (1,)))
    p = jax.nn.softmax(jnp.concatenate(logits, axis=-1), axis=-1)
    out, off = None, 0
    for k_, v_, _ in parts:
        n = k_.shape[2]
        o = jnp.einsum('bkgqs,bksd->bkgqd', p[..., off:off + n].astype(v_.dtype), v_)
        out = o if out is None else out + o
        off += n
    return out

def _ctx_attention(q, k, v, sink):
    qb = _q_blocks(q, k.shape[1], Q_BLOCK)
    o = lax.map(lambda qq: _attend(qq, ((k, v, None),), sink), qb)
    return _merge_blocks(o)

def _swa_latent(q, k, v, k_ctx, v_ctx, sink):
    T = q.shape[2]
    span = Q_BLOCK + 2 * SWA_WINDOW
    pad = ((0, 0), (0, 0), (SWA_WINDOW, SWA_WINDOW), (0, 0))
    kp, vp = jnp.pad(k, pad), jnp.pad(v, pad)
    qb = _q_blocks(q, k.shape[1], Q_BLOCK)

    def block(args):
        qq, j = args
        s = j * Q_BLOCK
        k_loc = lax.dynamic_slice_in_dim(kp, s, span, axis=2)
        v_loc = lax.dynamic_slice_in_dim(vp, s, span, axis=2)
        qpos = s + jnp.arange(Q_BLOCK)
        kpos = s - SWA_WINDOW + jnp.arange(span)
        valid = (jnp.abs(qpos[:, None] - kpos[None, :]) <= SWA_WINDOW) & (kpos[None, :] >= 0) & (kpos[None, :] < T)
        bias = jnp.where(valid, 0.0, NEG_INF).astype(jnp.float32)
        return _attend(qq, ((k_loc, v_loc, bias), (k_ctx, v_ctx, None)), sink)

    o = lax.map(block, (qb, jnp.arange(T // Q_BLOCK)))
    return _merge_blocks(o)

def _na_latent(q, k, v, k_ctx, v_ctx, rpb):
    H, T = q.shape[1], q.shape[2]
    rows = T // GRID_W
    kh = min(NA_KH, rows)
    cq = jnp.arange(GRID_W)
    cs = jnp.clip(cq - NA_KW // 2, 0, GRID_W - NA_KW)
    col_valid = (cq[None, :] >= cs[:, None]) & (cq[None, :] < cs[:, None] + NA_KW)
    dc = jnp.clip(cq[None, :] - cq[:, None], -(NA_KW - 1), NA_KW - 1) + (NA_KW - 1)
    mask = jnp.broadcast_to(col_valid[:, None, :], (GRID_W, kh, GRID_W)).reshape(GRID_W, kh * GRID_W)
    qb = _q_blocks(q, H, GRID_W)

    def block(args):
        qq, r = args
        rs = jnp.clip(r - kh // 2, 0, rows - kh)
        k_loc = lax.dynamic_slice_in_dim(k, rs * GRID_W, kh * GRID_W, axis=2)
        v_loc = lax.dynamic_slice_in_dim(v, rs * GRID_W, kh * GRID_W, axis=2)
        dr = rs + jnp.arange(kh) - r + (NA_KH - 1)
        tab = jnp.take(rpb, dr, axis=1)
        bias = tab[:, :, dc]
        bias = bias.transpose(0, 2, 1, 3).reshape(H, GRID_W, kh * GRID_W).astype(jnp.float32)
        bias = jnp.where(mask[None], bias, NEG_INF)[None, :, None]
        return _attend(qq, ((k_loc, v_loc, bias), (k_ctx, v_ctx, None)), None)

    o = lax.map(block, (qb, jnp.arange(rows)))
    return _merge_blocks(o)

def _mlstm_scan(q, k, v, ig, fg, C0, n0, m0):
    B, NH, T, DK = q.shape
    L = ML_CHUNK
    nc = T // L
    f32 = jnp.float32

    def chunks(a):
        return jnp.moveaxis(a.reshape(a.shape[:2] + (nc, L) + a.shape[3:]), 2, 0)

    qs = chunks(q.astype(f32) * DK ** -0.5)
    ks = chunks(k.astype(f32))
    vs = chunks(v.astype(f32))
    iss = chunks(ig.astype(f32))
    lfs = chunks(jax.nn.log_sigmoid(fg.astype(f32)))
    causal = jnp.tril(jnp.ones((L, L), dtype=bool))

    def step(carry, xs):
        C, n, m = carry
        qc, kc, vc, ic, lfc = xs
        b = jnp.cumsum(lfc, axis=-1)
        a = b + m[..., None]
        D = jnp.where(causal, b[..., :, None] - b[..., None, :] + ic[..., None, :], NEG_INF)
        m_t = jnp.maximum(a, jnp.max(D, axis=-1))
        w_inter = jnp.exp(a - m_t)
        S = jnp.einsum('bhtk,bhsk->bhts', qc, kc) * jnp.exp(D - m_t[..., None])
        num = w_inter[..., None] * jnp.einsum('bhtk,bhkv->bhtv', qc, C) + jnp.einsum('bhts,bhsv->bhtv', S, vc)
        den = w_inter * jnp.einsum('bhtk,bhk->bht', qc, n) + jnp.sum(S, axis=-1)
        h = num / jnp.maximum(jnp.abs(den), jnp.exp(-m_t))[..., None]
        bL = b[..., -1]
        m_new = m_t[..., -1]
        w_C = jnp.exp(bL + m - m_new)
        w_s = jnp.exp(bL[..., None] - b + ic - m_new[..., None])
        C_new = w_C[..., None, None] * C + jnp.einsum('bhs,bhsk,bhsv->bhkv', w_s, kc, vc)
        n_new = w_C[..., None] * n + jnp.einsum('bhs,bhsk->bhk', w_s, kc)
        return (C_new, n_new, m_new), h

    (C, n, m), h = lax.scan(step, (C0.astype(f32), n0.astype(f32), m0.astype(f32)),
                            (qs, ks, vs, iss, lfs))
    h = jnp.moveaxis(h, 0, 2).reshape(B, NH, T, -1)
    return h, C, n, m

def _mlstm_mixer(h, C0, n0, m0, w_up, conv_w, conv_b, w_qk, w_v, w_gate, b_gate, norm_w, skip, w_down):
    B, T, _ = h.shape
    xz = h @ w_up
    x_m, z = xz[..., :ML_D_IN], xz[..., ML_D_IN:]
    x_c = jax.nn.silu(_dwconv(x_m, conv_w, conv_b))
    qk = x_c @ w_qk
    q = _heads(qk[..., :ML_HEADS * ML_DK], ML_HEADS)
    k = _heads(qk[..., ML_HEADS * ML_DK:], ML_HEADS)
    v = _heads(x_m @ w_v, ML_HEADS)
    g = (x_m @ w_gate + b_gate).astype(jnp.float32).reshape(B, T, 2, 2, ML_HEADS).transpose(2, 3, 0, 4, 1)
    h_f, C_f, n_f, m_f = _mlstm_scan(q, k, v, g[0, 0], g[0, 1], C0[:, 0], n0[:, 0], m0[:, 0])
    h_b, C_b, n_b, m_b = _mlstm_scan(jnp.flip(q, 2), jnp.flip(k, 2), jnp.flip(v, 2),
                                     jnp.flip(g[1, 0], 2), jnp.flip(g[1, 1], 2),
                                     C0[:, 1], n0[:, 1], m0[:, 1])
    hs = h_f + jnp.flip(h_b, 2)
    mu = jnp.mean(hs, axis=-1, keepdims=True)
    var = jnp.mean(jnp.square(hs - mu), axis=-1, keepdims=True)
    hn = _unheads((hs - mu) * lax.rsqrt(var + NORM_EPS)).astype(h.dtype) * norm_w
    out = (hn + skip * x_c) * jax.nn.silu(z)
    return (out @ w_down, jnp.stack([C_f, C_b], axis=1), jnp.stack([n_f, n_b], axis=1),
            jnp.stack([m_f, m_b], axis=1))

def _conv_ffn(h, w_up, conv_w, conv_b, w_down):
    u = _dwconv(h @ w_up, conv_w, conv_b)
    g, val = u[..., :D_FF], u[..., D_FF:]
    return (jax.nn.silu(g) * val) @ w_down

def setup_inputs(seed: int = 0) -> dict:
    key = jax.random.key(seed)
    ks = iter(jax.random.split(key, 48))

    def nrm(shape, scale=1.0):
        return jax.random.normal(next(ks), shape, jnp.float32) * scale

    b_i = nrm((N_A, 2, 1, ML_HEADS), 0.1)
    b_f = 3.0 + nrm((N_A, 2, 1, ML_HEADS), 0.5)
    ml_b_gate = jnp.concatenate([b_i, b_f], axis=2).reshape(N_A, 4 * ML_HEADS)
    return {
        'x_prompt': nrm((BATCH, SEQ, D_MODEL)),
        'x_sample': nrm((DEC_BATCH, DEC_SEQ, D_MODEL)),
        'state_mlstm_C': nrm((DEC_BATCH, N_A, 2, ML_HEADS, ML_DK, ML_DV), 0.1),
        'state_mlstm_n': nrm((DEC_BATCH, N_A, 2, ML_HEADS, ML_DK), 0.5),
        'state_mlstm_m': nrm((DEC_BATCH, N_A, 2, ML_HEADS), 1.0),
        'cache_swa_k': nrm((DEC_BATCH, N_B, SWA_KV, PAST_LEN, HEAD_DIM)),
        'cache_swa_v': nrm((DEC_BATCH, N_B, SWA_KV, PAST_LEN, HEAD_DIM)),
        'cache_na_k': nrm((DEC_BATCH, N_C, NA_HEADS, PAST_LEN, HEAD_DIM)),
        'cache_na_v': nrm((DEC_BATCH, N_C, NA_HEADS, PAST_LEN, HEAD_DIM)),
        'c': nrm((DEC_BATCH, D_MODEL)),
        'c_ctx': nrm((D_MODEL,)),
        'ada_w': nrm((DEPTH, D_MODEL, 6 * D_MODEL), 0.5 * D_MODEL ** -0.5),
        'ada_b': nrm((DEPTH, 6 * D_MODEL), 0.02),
        'norm_w': 1.0 + nrm((DEPTH, 2, D_MODEL), 0.02),
        'final_norm_w': 1.0 + nrm((D_MODEL,), 0.02),
        'ffn_w_up': nrm((DEPTH, D_MODEL, 2 * D_FF), D_MODEL ** -0.5),
        'ffn_conv_w': nrm((DEPTH, FFN_CONV, 2 * D_FF), FFN_CONV ** -0.5),
        'ffn_conv_b': nrm((DEPTH, 2 * D_FF), 0.02),
        'ffn_w_down': nrm((DEPTH, D_FF, D_MODEL), D_FF ** -0.5),
        'ml_w_up': nrm((N_A, D_MODEL, 2 * ML_D_IN), D_MODEL ** -0.5),
        'ml_conv_w': nrm((N_A, ML_CONV, ML_D_IN), ML_CONV ** -0.5),
        'ml_conv_b': nrm((N_A, ML_D_IN), 0.02),
        'ml_w_qk': nrm((N_A, ML_D_IN, 2 * ML_HEADS * ML_DK), ML_D_IN ** -0.5),
        'ml_w_v': nrm((N_A, ML_D_IN, ML_HEADS * ML_DV), ML_D_IN ** -0.5),
        'ml_w_gate': nrm((N_A, ML_D_IN, 4 * ML_HEADS), 0.1 * ML_D_IN ** -0.5),
        'ml_b_gate': ml_b_gate,
        'ml_norm_w': 1.0 + nrm((N_A, ML_D_IN), 0.02),
        'ml_skip': 1.0 + nrm((N_A, ML_D_IN), 0.02),
        'ml_w_down': nrm((N_A, ML_D_IN, D_MODEL), ML_D_IN ** -0.5),
        'swa_w_qkv': nrm((N_B, D_MODEL, (SWA_HEADS + 2 * SWA_KV) * HEAD_DIM), D_MODEL ** -0.5),
        'swa_sink': nrm((N_B, SWA_HEADS), 0.5),
        'swa_w_o': nrm((N_B, SWA_HEADS * HEAD_DIM, D_MODEL), (SWA_HEADS * HEAD_DIM) ** -0.5),
        'na_w_qkv': nrm((N_C, D_MODEL, 3 * NA_HEADS * HEAD_DIM), D_MODEL ** -0.5),
        'na_rpb': nrm((N_C, NA_HEADS, 2 * NA_KH - 1, 2 * NA_KW - 1), 0.1),
        'na_w_o': nrm((N_C, NA_HEADS * HEAD_DIM, D_MODEL), (NA_HEADS * HEAD_DIM) ** -0.5),
    }

def reference(x_prompt, x_sample, state_mlstm_C, state_mlstm_n, state_mlstm_m,
              cache_swa_k, cache_swa_v, cache_na_k, cache_na_v, c, c_ctx,
              ada_w, ada_b, norm_w, final_norm_w,
              ffn_w_up, ffn_conv_w, ffn_conv_b, ffn_w_down,
              ml_w_up, ml_conv_w, ml_conv_b, ml_w_qk, ml_w_v, ml_w_gate, ml_b_gate,
              ml_norm_w, ml_skip, ml_w_down,
              swa_w_qkv, swa_sink, swa_w_o,
              na_w_qkv, na_rpb, na_w_o):
    xc, xl = x_prompt, x_sample
    Bp, Bd = xc.shape[0], xl.shape[0]
    sc = jax.nn.silu(c_ctx)
    sl = jax.nn.silu(c)
    C0 = jnp.zeros((Bp, 2, ML_HEADS, ML_DK, ML_DV), jnp.float32)
    n0 = jnp.zeros((Bp, 2, ML_HEADS, ML_DK), jnp.float32)
    m0 = jnp.zeros((Bp, 2, ML_HEADS), jnp.float32)
    new_C, new_n, new_m = [], [], []
    new_sk, new_sv, new_nk, new_nv = [], [], [], []

    for i in range(DEPTH):
        kind, j = i % N_MIXERS, i // N_MIXERS
        mod_c = (sc @ ada_w[i] + ada_b[i]).reshape(6, D_MODEL)
        mod_l = (sl @ ada_w[i] + ada_b[i]).reshape(Bd, 6, 1, D_MODEL)
        hc = _rmsnorm(xc, norm_w[i, 0]) * (1.0 + mod_c[1]) + mod_c[0]
        hl = _rmsnorm(xl, norm_w[i, 0]) * (1.0 + mod_l[:, 1]) + mod_l[:, 0]
        if kind == 0:
            oc, Cf, nf, mf = _mlstm_mixer(hc, C0, n0, m0, ml_w_up[j], ml_conv_w[j], ml_conv_b[j],
                                          ml_w_qk[j], ml_w_v[j], ml_w_gate[j], ml_b_gate[j],
                                          ml_norm_w[j], ml_skip[j], ml_w_down[j])
            ol, _, _, _ = _mlstm_mixer(hl, state_mlstm_C[:, j], state_mlstm_n[:, j], state_mlstm_m[:, j],
                                       ml_w_up[j], ml_conv_w[j], ml_conv_b[j],
                                       ml_w_qk[j], ml_w_v[j], ml_w_gate[j], ml_b_gate[j],
                                       ml_norm_w[j], ml_skip[j], ml_w_down[j])
            new_C.append(Cf)
            new_n.append(nf)
            new_m.append(mf)
        elif kind == 1:
            sink = swa_sink[j].reshape(SWA_KV, SWA_HEADS // SWA_KV)
            q_c, k_c, v_c = _split_qkv(hc, swa_w_qkv[j], SWA_HEADS, SWA_KV)
            oc = _unheads(_ctx_attention(q_c, k_c, v_c, sink)) @ swa_w_o[j]
            q_l, k_l, v_l = _split_qkv(hl, swa_w_qkv[j], SWA_HEADS, SWA_KV)
            ol = _unheads(_swa_latent(_axial_rope(q_l), _axial_rope(k_l), v_l,
                                      cache_swa_k[:, j], cache_swa_v[:, j], sink)) @ swa_w_o[j]
            new_sk.append(k_c)
            new_sv.append(v_c)
        else:
            q_c, k_c, v_c = _split_qkv(hc, na_w_qkv[j], NA_HEADS, NA_HEADS)
            oc = _unheads(_ctx_attention(q_c, k_c, v_c, None)) @ na_w_o[j]
            q_l, k_l, v_l = _split_qkv(hl, na_w_qkv[j], NA_HEADS, NA_HEADS)
            ol = _unheads(_na_latent(q_l, k_l, v_l, cache_na_k[:, j], cache_na_v[:, j], na_rpb[j])) @ na_w_o[j]
            new_nk.append(k_c)
            new_nv.append(v_c)
        xc = xc + mod_c[2] * oc
        xl = xl + mod_l[:, 2] * ol
        hc = _rmsnorm(xc, norm_w[i, 1]) * (1.0 + mod_c[4]) + mod_c[3]
        hl = _rmsnorm(xl, norm_w[i, 1]) * (1.0 + mod_l[:, 4]) + mod_l[:, 3]
        xc = xc + mod_c[5] * _conv_ffn(hc, ffn_w_up[i], ffn_conv_w[i], ffn_conv_b[i], ffn_w_down[i])
        xl = xl + mod_l[:, 5] * _conv_ffn(hl, ffn_w_up[i], ffn_conv_w[i], ffn_conv_b[i], ffn_w_down[i])

    y_prompt = _rmsnorm(xc, final_norm_w)
    y_sample = _rmsnorm(xl, final_norm_w)
    return (y_prompt, y_sample,
            jnp.stack(new_C, axis=1), jnp.stack(new_n, axis=1), jnp.stack(new_m, axis=1),
            jnp.stack(new_sk, axis=1), jnp.stack(new_sv, axis=1),
            jnp.stack(new_nk, axis=1), jnp.stack(new_nv, axis=1))


_drawn_inputs = setup_inputs


def setup_inputs(seed=0):
    import zlib

    import numpy as np

    out = dict(_drawn_inputs(seed))
    spreads = {}
    factors = {'state_mlstm_C': 4.373,
     'state_mlstm_n': 4.839,
     'state_mlstm_m': 4.418,
     'cache_swa_k': 2.861,
     'final_norm_w': 23.882,
     'ffn_conv_b': 15.304,
     'ml_norm_w': 34.855,
     'ml_skip': 24.794,
     'swa_sink': 26.11,
     'na_rpb': 29.408,
     'cache_na_k': 2.683}
    for name, (base, spread) in spreads.items():
        noise = np.random.default_rng([zlib.crc32(name.encode()), seed]).standard_normal(out[name].shape)
        drawn = base * np.exp(spread * noise) if base else spread * noise
        out[name] = jnp.asarray(drawn.astype(out[name].dtype))
    for name, factor in factors.items():
        out[name] = (out[name] * factor).astype(out[name].dtype)
    return out
```

```python
import numpy as np
import concourse.bass as bass
import concourse.mybir as mybir

F32 = mybir.dt.float32
F32R = mybir.dt.float32r
ALU = mybir.AluOpType
ACT = mybir.ActivationFunctionType
AX_X = mybir.AxisListType.X

P = 128
D = 1024
DEPTH = 4
T = 128
NS = 2
TOK = NS * T
KD = D // P
DFF = 2816
FB = 2 * DFF // P
NJ = DFF // 256
DIN = 2 * D
KI = DIN // P
MH = 4
DK = DIN // (2 * MH)
DV = DIN // MH
HD = 64
NH = D // HD
KV = NH // 4
EPS = 1e-6
NEG = -1e30

TILE = 2048
HALF = TILE // 2
RAW = 4
SPL = 4
MIXER = ["mlstm", "swa", "na", "mlstm"]
ML_INDEX = {0: 0, 3: 1}
ADA_PRE = 10
ADA_TILES = 24
SHIFT1, SCALE1, GATE1, SHIFT2, SCALE2, GATE2 = (4 * g for g in range(6))

_SMALL = [("ident", 128), ("mask_f", 128), ("mask_b", 128), ("na_mask", 128), ("ones", 1), ("cos", 64),
          ("sin", 64), ("ffn_conv_w", DEPTH * 3 * FB), ("ffn_conv_b", DEPTH * FB), ("norm_w", DEPTH * 2 * KD),
          ("ml_conv_w", 2 * 3 * KI), ("ml_conv_b", 2 * KI), ("ml_norm_w", 2 * KI), ("ml_skip", 2 * KI),
          ("n0", 2 * 16), ("m0", 2), ("b_gate", 2), ("gate_sel", 16), ("sink", NH), ("cond", 2 * KD)]
COL = {}
_at = 0
for _name, _n in _SMALL:
    COL[_name] = _at
    _at += _n
NSMALL = _at


def stream_order():
    order = [("ada", 0, g) for g in range(ADA_PRE)]
    for i in range(DEPTH):
        ada = [("ada", i, g) for g in range(ADA_PRE, ADA_TILES)]
        order += ada[0:2]
        if MIXER[i] == "mlstm":
            order += [("ml_x", i, t) for t in range(8)]
            order += [("ml_qk", i, g, k) for g in range(8) for k in range(2)]
            order += [("ml_v", i, c, t) for c in range(2) for t in range(8)]
            for h in range(MH):
                order += [ada[2 + 2 * h], ("ml_C", i, h), ada[3 + 2 * h]]
            order += [("ml_z", i, t) for t in range(8)]
            order += [("ml_down", i, t) for t in range(8)]
        elif MIXER[i] == "swa":
            order += [("q", i, t) for t in range(4)] + [("kv", i, t) for t in range(2)]
            order += ada[2:10]
            order += [("o", i, t) for t in range(4)]
        else:
            order += [("qkv", i, c, t) for c in range(3) for t in range(4)]
            order += ada[2:10]
            order += [("o", i, t) for t in range(4)]
        order += ada[10:14]
        order += [("ffn_up", i, 0), ("ffn_up", i, NJ)]
        for j in range(1, NJ):
            order += [("ffn_up", i, j), ("ffn_up", i, NJ + j), ("ffn_down", i, j - 1)]
            if i + 1 < DEPTH:
                order += [("ada", i + 1, j - 1)]
        order += [("ffn_down", i, NJ - 1)]
    return order


ORDER = stream_order()
NT = len(ORDER)
INDEX = {tile: n for n, tile in enumerate(ORDER)}


def ada_index(i, g):
    return ADA_TILES * i + g


def chunked(w, k0, nk, c0, nc):
    return w[k0 * P:(k0 + nk) * P, c0:c0 + nc].reshape(nk, P, nc).transpose(1, 0, 2).reshape(P, nk * nc)


def host_tile(tile, w):
    kind, i = tile[0], tile[1]
    j = ML_INDEX.get(i, 0)
    if kind == "ada":
        return chunked(w["ada_w"][i], 0, 8, 256 * tile[2], 256)
    if kind == "ml_x":
        return chunked(w["ml_w_up"][j], 0, 8, 256 * tile[2], 256)
    if kind == "ml_z":
        return chunked(w["ml_w_up"][j], 0, 8, DIN + 256 * tile[2], 256)
    if kind == "ml_qk":
        return chunked(w["ml_w_qk"][j], 8 * tile[3], 8, 256 * tile[2], 256)
    if kind == "ml_v":
        return chunked(w["ml_w_v"][j], 2 * tile[3], 2, 1024 * tile[2], 1024)
    if kind == "ml_C":
        c = w["state_mlstm_C"][0, j, :, tile[2]]
        return c.reshape(2, 2, P, DV).transpose(2, 0, 1, 3).reshape(P, TILE)
    if kind == "ml_down":
        return chunked(w["ml_w_down"][j], 2 * tile[2], 2, 0, 1024)
    if kind == "q":
        return chunked(w["swa_w_qkv"][0], 2 * tile[2], 2, 0, 1024)
    if kind == "kv":
        return chunked(w["swa_w_qkv"][0], 4 * tile[2], 4, 1024, 512)
    if kind == "qkv":
        return chunked(w["na_w_qkv"][0], 2 * tile[3], 2, 1024 * tile[2], 1024)
    if kind == "o":
        return chunked(w["swa_w_o" if MIXER[i] == "swa" else "na_w_o"][0], 2 * tile[2], 2, 0, 1024)
    if kind == "ffn_up":
        return chunked(w["ffn_w_up"][i], 0, 8, 256 * tile[2], 256)
    return chunked(w["ffn_w_down"][i], 2 * tile[2], 2, 0, 1024)


HEAD_ORDER = [4 * g + p // 2 + 2 * (p % 2) for g in range(NH // 4) for p in range(4)]


def columns(v):
    return np.asarray(v).reshape(-1, P).T


def host_arrays(w):
    f = np.float32
    stream = np.empty((NT, P, TILE), f)
    for n, tile in enumerate(ORDER):
        stream[n] = host_tile(tile, w)
    small = np.zeros((P, NSMALL), f)

    def put(name, a, rows=P):
        a = np.asarray(a, f)
        small[:rows, COL[name]:COL[name] + a.shape[1]] = a

    r = np.arange(P)
    put("ident", np.eye(P))
    put("mask_f", np.where(r[:, None] <= r[None, :], 0.0, NEG))
    put("mask_b", np.where(r[:, None] >= r[None, :], 0.0, NEG))
    col = r % 64
    start = np.clip(col - 8, 0, 64 - 16)
    ok = (col[None, :] >= start[:, None]) & (col[None, :] < start[:, None] + 16)
    put("na_mask", np.where(ok, 0.0, NEG))
    put("ones", np.ones((P, 1)))
    inv = np.power(f(10000.0), -np.arange(16, dtype=f) / f(16))
    ang = np.stack([(r // 64).astype(f)[:, None] * inv, col.astype(f)[:, None] * inv], 1)
    cos, sin = np.cos(ang), np.sin(ang)
    put("cos", np.stack([cos, cos], 2).reshape(P, 64))
    put("sin", np.stack([-sin, sin], 2).reshape(P, 64))
    put("ffn_conv_w", columns(w["ffn_conv_w"]))
    put("ffn_conv_b", columns(w["ffn_conv_b"]))
    put("norm_w", columns(w["norm_w"]))
    put("ml_conv_w", columns(w["ml_conv_w"]))
    put("ml_conv_b", columns(w["ml_conv_b"]))
    put("ml_norm_w", columns(w["ml_norm_w"]))
    put("ml_skip", columns(w["ml_skip"]))
    put("n0", columns(w["state_mlstm_n"][0]))
    for j in range(2):
        small[0:MH, COL["m0"] + j] = w["state_mlstm_m"][0, j, 0]
        small[32:32 + MH, COL["m0"] + j] = w["state_mlstm_m"][0, j, 1]
        small[0:16, COL["b_gate"] + j] = w["ml_b_gate"][j]
    sel = np.zeros((96, 16))
    for n, g in enumerate([GATE1 + k for k in range(4)] + [GATE2 + k for k in range(4)]):
        for s in range(NS):
            sel[4 * g + s, 2 * n + s] = sel[4 * g + 2 + s, 2 * n + s] = 1.0
    put("gate_sel", sel, 96)
    put("sink", np.broadcast_to(w["swa_sink"][0][HEAD_ORDER], (P, NH)))
    put("cond", np.stack([columns(w["c_ctx"]), columns(w["c"][0])], 2).reshape(P, 2 * KD))
    ada_b = np.zeros((DEPTH, ADA_TILES, 4, 256), f)
    ada_b[:, :, 0:2] = w["ada_b"].reshape(DEPTH, ADA_TILES, 1, 256)
    dq = np.arange(T)
    dr = (dq // 64)[None, :] - (dq // 64)[:, None] + 7
    dc = np.clip((dq % 64)[None, :] - (dq % 64)[:, None], -15, 15) + 15
    rpb = w["na_rpb"][0][HEAD_ORDER][:, dr, dc]
    return {
        "stream": stream, "small": small,
        "x": np.concatenate([w["x_prompt"][0], w["x_sample"][0]], 1),
        "ada_b": ada_b.reshape(DEPTH, 96, 256),
        "w_gate": np.stack([chunked(w["ml_w_gate"][j], 0, KI, 0, 16) for j in range(2)]),
        "rpb": np.ascontiguousarray(rpb.transpose(1, 0, 2)).reshape(T, NH * T),
        "final_w": np.broadcast_to(w["final_norm_w"], (P, D)),
        "swa_cache": np.concatenate([np.repeat(w[n][0, 0].transpose(1, 0, 2), 2, axis=1).reshape(T, 2 * KV * HD)
                                     for n in ("cache_swa_k", "cache_swa_v")], 1),
        "na_cache": np.concatenate([w["cache_na_k"][0, 0].transpose(1, 0, 2).reshape(T, D),
                                    w["cache_na_v"][0, 0].transpose(1, 0, 2).reshape(T, D)], 1),
    }


OUTPUTS = [("y_prompt", (1, T, D)), ("y_sample", (1, T, D)), ("new_C", (1, 2, 2, MH, DK, DV)),
           ("new_n", (1, 2, 2, MH, DK)), ("new_m", (1, 2, 2, MH)),
           ("swa_k", (1, 1, KV, T, HD)), ("swa_v", (1, 1, KV, T, HD)),
           ("na_k", (1, 1, NH, T, HD)), ("na_v", (1, 1, NH, T, HD))]


def build(nc, io):
    base = (nc.sbuf_base + 63) // 64 * 64
    KB = 1024

    def sb(name, cols, dt, at, rows=P):
        return nc.alloc_sbuf_tensor_at(name, [rows, cols], dt, offset=base + at)

    raw = [sb(f"raw{r}", TILE, F32, 8 * KB * r) for r in range(RAW)]
    spl_hi = [sb(f"spl_hi{r}", HALF, F32R, 32 * KB + 4 * KB * r) for r in range(SPL)]
    spl_lo = [sb(f"spl_lo{r}", HALF, F32R, 48 * KB + 4 * KB * r) for r in range(SPL)]
    x = sb("x", NS * D, F32, 64 * KB)
    H_hi = sb("H_hi", KD * TOK, F32R, 72 * KB)
    H_lo = sb("H_lo", KD * TOK, F32R, 80 * KB)
    rA, rB, rX, rT, rW = 88 * KB, 120 * KB, 152 * KB, 168 * KB, 184 * KB
    A_hi = sb("A_hi", KI * TOK, F32R, rA)
    A_lo = sb("A_lo", KI * TOK, F32R, rA + 16 * KB)
    B_hi = sb("B_hi", KI * TOK, F32R, rB)
    B_lo = sb("B_lo", KI * TOK, F32R, rB + 16 * KB)
    XCS = sb("XCS", KI * TOK, F32, rX)
    v = sb("v", NS * DIN, F32, rB)
    ST = sb("ST", MH * TOK, F32, rB + 16 * KB)
    knat = sb("knat", D, F32, rB + 20 * KB)
    c_stage = sb("c_stage", TILE, F32, rB + 24 * KB)
    E = sb("E", 2 * TOK, F32, rA)
    Pw = sb("Pw", 2 * TOK, F32, rA + 2 * KB)
    Em = sb("Em", 2 * TOK, F32, rA + 4 * KB)
    den = sb("den", 2 * TOK, F32, rA + 6 * KB)
    PT = sb("PT", TOK, F32, rA + 8 * KB)
    qs = sb("qs", 4 * T, F32, rA + 9 * KB)
    qs_hi = sb("qs_hi", 4 * T, F32R, rA + 11 * KB)
    qs_lo = sb("qs_lo", 4 * T, F32R, rA + 13 * KB)
    hn = sb("hn", NS * DV, F32, rA + 15 * KB)
    kw = sb("kw", 2 * DK, F32, rA + 19 * KB)
    xn = sb("xn", NS * D, F32, rT)
    hf = [sb(f"hf{b}", 2 * TOK, F32, rT + 8 * KB + 2 * KB * b) for b in range(2)]
    wg_raw = sb("wg_raw", KI * 16, F32, rT)
    wg_hi = sb("wg_hi", KI * 16, F32R, rT + 1 * KB)
    wg_lo = sb("wg_lo", KI * 16, F32R, rT + 2 * KB)
    Q = sb("Q", KD * TOK, F32, rT)
    K = sb("K", KD * TOK, F32, rT + 8 * KB)
    gate_bc = sb("gate_bc", NS * D, F32, rT + 8 * KB)
    t1 = [sb(f"t1_{b}", 2 * TOK, F32, rW + 2 * KB * b) for b in range(2)]
    ow = [sb(f"ow{b}", 2 * TOK, F32, rW + 4 * KB + 2 * KB * b) for b in range(2)]
    tg = sb("tg", 2 * TOK, F32, rX)
    tv = sb("tv", 2 * TOK, F32, rX + 2 * KB)
    sg = sb("sg", 2 * TOK, F32, rX + 4 * KB)
    gt = sb("gt", 2 * TOK, F32, rX + 6 * KB)
    G_hi = sb("G_hi", 2 * TOK, F32R, rX + 8 * KB)
    G_lo = sb("G_lo", 2 * TOK, F32R, rX + 10 * KB)
    qrow = sb("qrow", NS * D, F32, rA)
    krow = sb("krow", NS * D, F32, rA + 8 * KB)
    vrow = sb("vrow", NS * D, F32, rA + 16 * KB)
    rope_t = sb("rope_t", D, F32, rA + 24 * KB)
    rope_u = sb("rope_u", D, F32, rA + 28 * KB)
    qT = sb("qT", KD * TOK, F32, rB)
    kT = sb("kT", KD * 3 * T, F32, rB + 8 * KB)
    cache = sb("cache", 2 * D, F32, rB + 20 * KB)
    Ea = sb("Ea", 4 * TOK, F32, rB + 28 * KB)
    Sa = sb("Sa", 4 * TOK, F32, rX)
    PTa = sb("PTa", 4 * TOK, F32, rX + 4 * KB)
    bias = sb("bias", NH * T, F32, rX + 8 * KB)
    fw = sb("fw", D, F32, rB)
    mod_row = sb("mod_row", ADA_PRE * 256, F32, rB + 4 * KB)
    at = 192 * KB

    def small_sb(name, cols, dt=F32, rows=P):
        nonlocal at
        t = sb(name, cols, dt, at, rows)
        at += (cols * 4 + 63) // 64 * 64
        return t

    small = small_sb("small", NSMALL)
    mod_stage = small_sb("mod_stage", 256)
    mod_raw = small_sb("mod_raw", 256)
    ada_b = small_sb("ada_b", 256)
    mod_b = small_sb("mod_b", 256)
    modT = small_sb("modT", 192)
    coef_a = small_sb("coef_a", KD * NS)
    coef_b = small_sb("coef_b", KD * NS)
    cond = small_sb("cond", KD * NS)
    cond_parts = small_sb("cond_parts", KD * 4, F32R)
    ssq = small_sb("ssq", NS)
    var = small_sb("var", NS)
    rstd = small_sb("rstd", NS)
    half_pow = small_sb("half_pow", NS)
    bn = small_sb("bn", NS * 6)
    mv = small_sb("mv", NS * 2)
    ccol = small_sb("ccol", NS * 36)
    gI, gF, gA, gM, gb, gc, gG = (small_sb(n, TOK) for n in ("gI", "gF", "gA", "gM", "gb", "gc", "gG"))
    g16 = small_sb("g16", TOK)
    gz = small_sb("gz", T)
    RB = small_sb("RB", 2 * TOK)
    RBW = small_sb("RBW", T)
    n_out = small_sb("n_out", 2 * DK)
    m_out = small_sb("m_out", 1)
    nsink = small_sb("nsink", NH)
    mx = small_sb("mx", 4)
    nm = small_sb("nm", 4)
    sums = small_sb("sums", 4)
    esink = small_sb("esink", 4)
    rsum = small_sb("rsum", 4)
    credit = small_sb("credit", 8)
    assert base + at <= nc.sbuf_usable_end, (base, at)

    ps = [nc.alloc_psum_tensor(f"ps{b}", [P, 512], F32) for b in range(8)]
    ACC, UP, ADA_PS, MISC = ps[0:4], ps[4:6], ps[6], ps[7]

    def sc(name, k=0, n=1, rows=P, r0=0):
        return small[r0:r0 + rows, COL[name] + k:COL[name] + k + n]

    ident = small[:, COL["ident"]:COL["ident"] + P]

    def v3(ap, b):
        return ap.rearrange("p (a b) -> p a b", b=b)

    names = """raw0 raw1 raw2 raw3 hi_done lo_done half_used
        loads x_loaded cond_silu cond_hi cond_lo misc_init
        ada_evac mod_landed adab_landed modb_done modT_mm modT_done gate_mm gate_evac
        ssq_done pool_chain rstd_done xn_done nt_done hf_done hhi_done h_done x_done dve_link act_link
        xm_hi t1_done conv_half conv_done xc_done xc_hi xc_lo xcs_done
        wg_landed wg_hi_done wg_done gates_mm g16_done rows_landed row_dve row_act c_mm
        qk_evac st_mm st_evac v_evac_a v_evac_d
        bc_mm arg_done e_done em_done qs_done p_done den_mm qs2_done qs_hi_done pt_done num_mm var_done
        rstd2_done hn_done ht_mm hc_done kw_done cn_mm cn_evac n_mm n_evac c_landed n_landed m_done m_landed
        z_silu z_mul z_hi z_lo
        tg_done cg_half cg_done tv_done cv_half cv_done sg_done gt_done ghi_done glo_done
        cache_landed bias_landed bias_done row_q_a row_q_d row_k row_v roped tq_mm tq_evac tk_mm tk_evac kv_landed
        s_mm nm_done exp_done esink_in esink_done pn_done pt_mm pt_evac o_mm o_hi o_lo
        fw_landed final_done y_landed""".split()
    S = {n: nc.alloc_semaphore(n) for n in names}
    raw_landed = [S[f"raw{r}"] for r in range(RAW)]

    def split_hi(act, n, adv=0):
        if n >= NT:
            return
        act.wait_ge(raw_landed[n % RAW], 16 * (n // RAW + 1) + adv * 4)
        for h in range(2):
            m = 2 * n + h
            if m >= SPL:
                act.wait_ge(S["half_used"], m - SPL + 1 + adv * 2)
            act.activation(spl_hi[m % SPL][:, :], raw[n % RAW][:, h * HALF:(h + 1) * HALF],
                           ACT.Copy).then_inc(S["hi_done"], 1)

    def split_lo(dve, n, adv=0):
        if n >= NT:
            return
        for h in range(2):
            m = 2 * n + h
            dve.wait_ge(S["hi_done"], m + 1 + adv * 2)
            dve.tensor_tensor(spl_lo[m % SPL][:, :], raw[n % RAW][:, h * HALF:(h + 1) * HALF],
                              spl_hi[m % SPL][:, :].bitcast(F32), ALU.subtract).then_inc(S["lo_done"], 1)

    def tile_used(eng, n, adv=0):
        eng.wait_ge(S["half_used"], 2 * n + 2 + adv * 2)

    def out_half(t, g, s, e):
        return t[HD * e:HD * e + HD, 2 * g * TOK:(2 * g + 2) * TOK].rearrange("p (a s t) -> p a s t", s=2,
                                                                              t=T)[:, :, s, :]

    def psum_half(e):
        return UP[0][HD * e:HD * e + HD, :].rearrange("p (a e t) -> p a e t", e=2, t=T)[:, :, e, :]

    class Link:
        def __init__(self, eng, name):
            self.eng, self.sem, self.n = eng, S[name], 0

        def __call__(self, ins):
            ins.then_inc(self.sem, 1)
            self.n += 1

        def wait(self):
            self.eng.wait_ge(self.sem, self.n)

    with nc.Block() as block:

        @block.sync
        def _(sp):
            for n in range(RAW):
                sp.dma_start(raw[n][:, :], io["stream"][n]).then_inc(raw_landed[n], 16)

            def refill(n, adv=0):
                sp.wait_ge(S["lo_done"], 2 * (n - RAW) + 2 + adv * 2)
                src = io["stream"][n] if isinstance(adv, int) else \
                    io["stream"][bass.ds(adv + n, 1)].rearrange("a p n -> p (a n)")
                sp.dma_start(raw[n % RAW][:, :], src).then_inc(raw_landed[n % RAW], 16)

            rounds = NT // RAW - 1
            with sp.Fori(0, rounds) as it:
                for r in range(RAW):
                    refill(RAW + r, it * RAW)
            for n in range((rounds + 1) * RAW, NT):
                refill(n)

        @block.tensor
        def _(pe):
            def weights_stationary(n, adv, chunk, k0, bank, first, last):
                for h in range(2):
                    m = 2 * n + h
                    pe.wait_ge(S["lo_done"], m + 1 + adv * 2)
                    for b in range(2):
                        for k in range(4):
                            c = slice(k * 256 + b * P, k * 256 + b * P + P)
                            w_hi, w_lo = spl_hi[m % SPL][:, c], spl_lo[m % SPL][:, c]
                            x_hi, x_lo = chunk(k0 + 4 * h + k)
                            out = bank[:, b * TOK:(b + 1) * TOK]
                            st = first and h == 0 and b == 0 and k == 0
                            en = last and h == 1 and b == 1 and k == 3
                            pe.matmul(out, w_hi, x_hi, start=st, stop=False, skip_group_check=True)
                            pe.matmul(out, w_hi, x_lo, start=False, stop=False, skip_group_check=True)
                            mm = pe.matmul(out, w_lo, x_hi, start=False, stop=en, skip_group_check=True)
                    mm.then_inc(S["half_used"], 1)

            def rows_stationary(n, adv, chunk, first, last, width=1024, banks=None):
                for h in range(2):
                    m = 2 * n + h
                    pe.wait_ge(S["lo_done"], m + 1 + adv * 2)
                    per = HALF // width
                    for k in range(per):
                        for s in range(NS):
                            a_hi, a_lo = chunk(per * h + k, s)
                            for a, parts in ((a_hi, (spl_hi, spl_lo)), (a_lo, (spl_hi,))):
                                for w in parts:
                                    for c in range(width // 512):
                                        out = (banks or ACC)[s * (width // 512) + c]
                                        st = first and h == 0 and k == 0 and a is a_hi and w is spl_hi
                                        en = last and h == 1 and k == per - 1 and a is a_lo
                                        o = k * width + c * 512
                                        mm = pe.matmul(out[:, :], a, w[m % SPL][:, o:o + 512], start=st, stop=en,
                                                       skip_group_check=True)
                    mm.then_inc(S["half_used"], 1)

            def ada(n, i, g, adv=0, more=0):
                if ada_index(i, g):
                    pe.wait_ge(S["ada_evac"], ada_index(i, g) + more)
                for h in range(2):
                    m = 2 * n + h
                    pe.wait_ge(S["lo_done"], m + 1 + adv * 2)
                    for k in range(4):
                        c = cond_parts[:, 4 * (4 * h + k):4 * (4 * h + k) + 4]
                        for w in (spl_hi, spl_lo):
                            mm = pe.matmul(ADA_PS[0:4, 0:256], c, w[m % SPL][:, k * 256:(k + 1) * 256],
                                           start=h == 0 and k == 0 and w is spl_hi,
                                           stop=h == 1 and k == 3 and w is spl_lo)
                    mm.then_inc(S["half_used"], 1)

            def col(t, k, s=None):
                o = k * TOK + (0 if s is None else s * T)
                return t[:, o:o + (TOK if s is None else T)]

            def both(hi, lo):
                return lambda k, s=None: (col(hi, k, s), col(lo, k, s))

            def norm(q, tiles):
                i = q // 2
                rows = 32 if q % 2 == 0 else 96
                pe.wait_ge(S["modb_done"], 3 * i + (1 if q % 2 == 0 else 2))
                for a in range(2):
                    mm = pe.transpose(MISC[:, a * 96:a * 96 + rows], mod_b[0:rows, a * P:(a + 1) * P],
                                      ident[0:rows, 0:rows])
                mm.then_inc(S["modT_mm"], 1)
                for n in tiles:
                    ada(n, i, ORDER[n][2])
                pe.wait_ge(S["xn_done"], 2 * q + 2)
                for g in range(4):
                    for k in range(2):
                        for s in range(NS):
                            o = (k * 2 + s) * T
                            mm = pe.transpose(ACC[g][:, o:o + T],
                                              xn[:, s * D + (2 * g + k) * P:s * D + (2 * g + k + 1) * P], ident)
                    mm.then_inc(S["nt_done"], 1)
                pe.wait_ge(S["h_done"], 4 * q + 4)

            def gates(r):
                pe.wait_ge(S["modT_done"], r + 1)
                pe.wait_ge(S["modb_done"], 3 * (r // 2) + 2 + r % 2)
                if MIXER[r // 2] == "mlstm":
                    pe.wait_ge(S["n_evac"], MH * (ML_INDEX[r // 2] + 1))
                for s in range(NS):
                    for c in range(2):
                        b = 4 * r + 2 * s + c
                        if b:
                            pe.wait_ge(S["gate_evac"], b)
                        for k in range(2):
                            sel = sc("gate_sel", 2 * (4 * (r % 2) + 2 * c + k) + s, rows=96).to_broadcast([96, P])
                            mm = pe.matmul(MISC[:, k * 256:(k + 1) * 256], sel, mod_b[0:96, :],
                                           start=k == 0, stop=k == 1, skip_group_check=True)
                        mm.then_inc(S["gate_mm"], 1)

            def mlstm(i):
                j = ML_INDEX[i]
                n0 = INDEX["ml_x", i, 0]
                with pe.Fori(0, 2) as it:
                    for t in range(4):
                        pe.wait_ge(S["conv_done"], 8 * j + t + 1 + it * 4)
                        weights_stationary(n0 + t, it * 4, both(H_hi, H_lo), 0, UP[t % 2], True, True)
                pe.wait_ge(S["wg_done"], j + 1)
                pe.wait_ge(S["xc_lo"], 2 + 8 * (j + 1))
                for k in range(KI):
                    w_hi, w_lo = wg_hi[:, 16 * k:16 * k + 16], wg_lo[:, 16 * k:16 * k + 16]
                    a_hi, a_lo = both(A_hi, A_lo)(k)
                    pe.matmul(MISC[0:16, 0:TOK], w_hi, a_hi, start=k == 0, stop=False)
                    pe.matmul(MISC[0:16, 0:TOK], w_hi, a_lo, start=False, stop=False)
                    mm = pe.matmul(MISC[0:16, 0:TOK], w_lo, a_hi, start=False, stop=k == KI - 1)
                mm.then_inc(S["gates_mm"], 1)
                n0 = INDEX["ml_qk", i, 0, 0]
                for part in range(2):
                    with pe.Fori(0, 2) as it:
                        for t in range(4):
                            if t % 2 == 0:
                                pe.wait_ge(S["qk_evac"], 8 * j + 4 * part + t // 2 + 1 + it * 2)
                            weights_stationary(n0 + 8 * part + t, it * 4, both(B_hi, B_lo), 8 * (t % 2),
                                               UP[(t // 2) % 2], t % 2 == 0, t % 2 == 1)
                pe.wait_ge(S["qk_evac"], 2 + 8 * (j + 1))
                for b in range(2):
                    for hs in range(4 * b, 4 * b + 4):
                        h, s = hs // 2, hs % 2
                        for c in range(2):
                            mm = pe.matmul(ACC[b][:, (hs % 4) * T:(hs % 4 + 1) * T], col(K, 2 * h + c, s),
                                           col(Q, 2 * h + c, s), start=hs % 4 == 0 and c == 0, stop=c == 1,
                                           skip_group_check=True)
                    mm.then_inc(S["st_mm"], 1)
                for b in range(2):
                    for c in range(4):
                        mm = pe.transpose(ACC[2 + b][:, c * P:(c + 1) * P], col(K, 4 * b + c, 0), ident)
                    mm.then_inc(S["st_mm"], 1)
                pe.wait_ge(S["row_dve"], ROW_DVE * j + ROW_C)
                for s in range(NS):
                    mm = pe.transpose(MISC[:, 36 * s:36 * s + 36], gc[0:36, s * T:(s + 1) * T], ident[0:36, 0:36])
                mm.then_inc(S["c_mm"], 1)
                n0 = INDEX["ml_v", i, 0, 0]
                for half in range(2):
                    if half == 0:
                        pe.wait_ge(S["st_evac"], 4 * (j + 1))
                    else:
                        pe.wait_ge(S["v_evac_a"], 4 * j + 2)
                        pe.wait_ge(S["v_evac_d"], 4 * j + 2)
                    for t in range(8):
                        rows_stationary(n0 + 8 * half + t, 0, lambda k, s: both(A_hi, A_lo)(2 * t + k, s),
                                        t == 0, t == 7)
                for h in range(MH):
                    head(i, j, h)
                n0 = INDEX["ml_z", i, 0]
                pe.wait_ge(S["hc_done"], 4 * (j + 1))
                with pe.Fori(0, 2) as it:
                    for t in range(4):
                        pe.wait_ge(S["z_silu"], 8 * j + t + 1 + it * 4)
                        weights_stationary(n0 + t, it * 4, both(H_hi, H_lo), 0, UP[t % 2], True, True)
                gates(2 * i)
                pe.wait_ge(S["z_lo"], 2 + 8 * (j + 1))
                n0 = INDEX["ml_down", i, 0]
                for t in range(8):
                    rows_stationary(n0 + t, 0, lambda k, s: both(A_hi, A_lo)(2 * t + k, s), t == 0, t == 7)

            def head(i, j, h):
                q = 4 * j + h
                n = INDEX["ml_C", i, h]
                if q:
                    pe.wait_ge(S["hc_done"], q)
                    pe.wait_ge(S["n_evac"], q)
                if h == 0:
                    pe.wait_ge(S["v_evac_a"], 4 * (j + 1))
                    pe.wait_ge(S["v_evac_d"], 4 * (j + 1))
                    pe.wait_ge(S["row_dve"], ROW_DVE * (j + 1))
                    pe.wait_ge(S["row_act"], ROW_ACT * (j + 1))
                pe.matmul(UP[0][:, :], ident[0:36, h:h + 1].to_broadcast([36, P]), RB[0:36, :], start=True, stop=True)
                pe.matmul(UP[1][:, :], ident[0:36, 32 + h:33 + h].to_broadcast([36, P]), RB[0:36, :],
                          start=True, stop=True)
                for d in range(2):
                    mm = pe.matmul(ACC[0][:, d * T:(d + 1) * T],
                                   ident[0:36, 32 * d + h:32 * d + h + 1].to_broadcast([36, P]), RBW[0:36, :],
                                   start=d == 0, stop=d == 1, skip_group_check=True)
                mm.then_inc(S["bc_mm"], 1)
                ada(n - 1, i, ORDER[n - 1][2])
                pe.wait_ge(S["p_done"], q + 1)
                pe.wait_ge(S["qs_done"], q + 1)
                pe.matmul(ACC[1][:, :], sc("ones").to_broadcast([P, P]), Pw[:, :], start=True, stop=False,
                          skip_group_check=True)
                for d in range(2):
                    for c in range(2):
                        o = 16 * j + (4 * d + h) * 2 + c
                        mm = pe.matmul(ACC[1][:, (2 * d + 1) * T:(2 * d + 2) * T],
                                       sc("n0", o).to_broadcast([P, P]), qs[:, (2 * d + c) * T:(2 * d + c + 1) * T],
                                       start=False, stop=d == 1 and c == 1, skip_group_check=True)
                mm.then_inc(S["den_mm"], 1)
                pe.wait_ge(S["pt_done"], q + 1)
                pe.matmul(ACC[0][:, :], PT[:, 0:T], v[:, h * DV:(h + 1) * DV], start=True, stop=True)
                pe.wait_ge(S["qs_hi_done"], q + 1)
                pe.wait_ge(S["qs2_done"], 2 * q + 2)
                pe.matmul(ACC[1][:, :], PT[:, T:TOK], v[:, DIN + h * DV:DIN + (h + 1) * DV], start=True, stop=False,
                          skip_group_check=True)
                for d in range(2):
                    m = 2 * n + d
                    pe.wait_ge(S["lo_done"], m + 1)
                    for c in range(2):
                        o = slice((2 * d + c) * T, (2 * d + c + 1) * T)
                        for a, w in ((qs_hi, spl_hi), (qs_hi, spl_lo), (qs_lo, spl_hi)):
                            mm = pe.matmul(ACC[1][:, :], a[:, o], w[m % SPL][:, c * DV:(c + 1) * DV], start=False,
                                           stop=d == 1 and c == 1 and a is qs_lo, skip_group_check=True)
                    mm.then_inc(S["half_used"], 1)
                pe.wait_ge(S["kw_done"], 2 * q + 2)
                for d in range(2):
                    for c in range(2):
                        e = 4 * q + 2 * d + c
                        if e >= 2:
                            pe.wait_ge(S["cn_evac"], e - 1)
                        pe.matmul(ACC[2 + c][:, :], kw[:, d * DK + c * P:d * DK + (c + 1) * P],
                                  v[:, h * DV:(h + 1) * DV], start=True, stop=True).then_inc(S["cn_mm"], 1)
                for d in range(2):
                    last = d * TOK + (T - 1 if d == 0 else 0)
                    mm = pe.matmul(MISC[0:1, d * DK:(d + 1) * DK], E[:, last:last + 1],
                                   knat[:, h * DK:(h + 1) * DK], start=d == 0, stop=d == 1, skip_group_check=True)
                mm.then_inc(S["n_mm"], 1)
                ada(n + 1, i, ORDER[n + 1][2])
                pe.wait_ge(S["hn_done"], 2 * q + 2)
                for f in range(4):
                    for s in range(NS):
                        o = ((f % 2) * 2 + s) * T
                        mm = pe.transpose(UP[f // 2][:, o:o + T], hn[:, s * DV + f * P:s * DV + (f + 1) * P], ident)
                mm.then_inc(S["ht_mm"], 1)

            def attention(i):
                a = i - 1
                nb = 4 if a == 0 else 8
                if a == 0:
                    n0 = INDEX["q", i, 0]
                    for t in range(4):
                        rows_stationary(n0 + t, 0, lambda k, s: both(H_hi, H_lo)(2 * t + k, s), t == 0, t == 3)
                    n0 = INDEX["kv", i, 0]
                    for t in range(2):
                        rows_stationary(n0 + t, 0, lambda k, s: both(H_hi, H_lo)(4 * t + k, s), t == 0, t == 1,
                                        width=512, banks=UP)
                else:
                    for c in range(3):
                        if c:
                            pe.wait_ge(S["row_q_a"], 2 + 2 * c)
                            pe.wait_ge(S["row_q_d"], 2 + 2 * c)
                        n0 = INDEX["qkv", i, c, 0]
                        for t in range(4):
                            rows_stationary(n0 + t, 0, lambda k, s: both(H_hi, H_lo)(2 * t + k, s), t == 0, t == 3)
                pe.wait_ge(S["row_q_a"], 2 if a == 0 else 8)
                pe.wait_ge(S["row_q_d"], 2 if a == 0 else 8)
                pe.wait_ge(S["roped"], 1)
                for b in range(4):
                    for p in range(4):
                        pr, s = 2 * b + p // 2, p % 2
                        mm = pe.transpose(ACC[b][:, p * T:(p + 1) * T], qrow[:, s * D + pr * P:s * D + (pr + 1) * P],
                                          ident)
                    mm.then_inc(S["tq_mm"], 1)
                pe.wait_ge(S["roped"], 2)
                pe.wait_ge(S["cache_landed"], 16 * (a + 1))
                for b in range(3 * nb // 4):
                    bank = (UP + [ADA_PS, MISC])[b % 2]
                    if b >= 2:
                        pe.wait_ge(S["tk_evac"], 3 * a + b - 1)
                    elif a == 0:
                        pe.wait_ge(S["row_k"], 2)
                        pe.wait_ge(S["row_v"], 2)
                    for p in range(4):
                        blk, src = divmod(4 * b + p, 3)
                        rows = cache[:, blk * P:(blk + 1) * P] if src == 2 else \
                            krow[:, src * nb * P + blk * P:src * nb * P + (blk + 1) * P]
                        mm = pe.transpose(bank[:, p * T:(p + 1) * T], rows, ident)
                    mm.then_inc(S["tk_mm"], 1)
                pe.wait_ge(S["tq_evac"], 4 * (a + 1))
                pe.wait_ge(S["tk_evac"], 3 * a + 3 * nb // 4)
                n = INDEX["ada", i, ADA_PRE + 2]
                for u in range(8):
                    g, s = u // 2, u % 2
                    w = 8 * a + u
                    if w:
                        pe.wait_ge(S["exp_done"], 4 * w)
                    if w and a == 1:
                        pe.wait_ge(S["nm_done"], w)
                    width = (1 + s) * T
                    for p in range(4):
                        hd = HEAD_ORDER[4 * g + p]
                        r0 = HD * (hd % 2)
                        blk = hd // 4 if a == 0 else hd // 2
                        q_ = qT[r0:r0 + HD, (hd // 2) * TOK + s * T:(hd // 2) * TOK + (s + 1) * T]
                        mm = pe.matmul(ACC[p // 2][:, (p % 2) * width:(p % 2 + 1) * width], q_,
                                       kT[r0:r0 + HD, blk * 3 * T + s * T:blk * 3 * T + s * T + width],
                                       start=p % 2 == 0, stop=p % 2 == 1, skip_group_check=True)
                    mm.then_inc(S["s_mm"], 1)
                    ada(n + u, i, ORDER[n + u][2])
                    pe.wait_ge(S["pn_done"], w + 1)
                    for b in range(1 + s):
                        for p in range(4):
                            o = (4 * b + p) * T
                            mm = pe.transpose(ACC[2 + b][:, p * T:(p + 1) * T], Ea[:, o:o + T], ident)
                        mm.then_inc(S["pt_mm"], 1)
                    pe.wait_ge(S["pt_evac"], 3 * (w // 2) + 1 + 2 * s)
                    if w:
                        pe.wait_ge(S["o_lo"], 2 * w)
                    for p in range(4):
                        hd = HEAD_ORDER[4 * g + p]
                        k = hd % 4
                        blk = hd // 4 if a == 0 else hd // 2
                        for e in range(1 + s):
                            o = (p * (1 + s) + e) * T
                            vals = cache[:, (nb + blk) * P:(nb + blk + 1) * P] if e else \
                                vrow[:, s * nb * P + blk * P:s * nb * P + (blk + 1) * P]
                            mm = pe.matmul(UP[0][:, k * T:(k + 1) * T], vals, PTa[:, o:o + T],
                                           start=p == 0 and e == 0, stop=e == s, skip_group_check=True)
                    mm.then_inc(S["o_mm"], 1)
                gates(2 * i)
                pe.wait_ge(S["o_lo"], 16 * (a + 1))
                n0 = INDEX["o", i, 0]
                for t in range(4):
                    rows_stationary(n0 + t, 0, lambda k, s: both(H_hi, H_lo)(2 * t + k, s), t == 0, t == 3)

            def ffn(i):
                n0 = INDEX["ffn_up", i, 0]
                mine = lambda k, s: (col(G_hi, k, s), col(G_lo, k, s))

                def step(j, n, adv, jj, with_ada):
                    if NJ * i + j > 0:
                        pe.wait_ge(S["cg_done"], NJ * i + j + jj)
                        pe.wait_ge(S["cv_done"], NJ * i + j + jj)
                    weights_stationary(n, adv, both(H_hi, H_lo), 0, UP[0], True, True)
                    weights_stationary(n + 1, adv, both(H_hi, H_lo), 0, UP[1], True, True)
                    if j > 0:
                        pe.wait_ge(S["glo_done"], NJ * i + j + jj)
                        rows_stationary_ffn(n + 2, adv, mine, j == 1 and isinstance(jj, int), False)
                    if with_ada:
                        ada(n + 3, i + 1, j - 1, adv, jj)

                def rows_stationary_ffn(n, adv, chunk, first, last):
                    rows_stationary(n, adv, chunk, first, last)

                step(0, n0, 0, 0, False)
                step(1, n0 + 2, 0, 0, i + 1 < DEPTH)
                if i + 1 < DEPTH:
                    with pe.Fori(0, NJ - 2) as it:
                        step(2, n0 + 6, it * 4, it, True)
                else:
                    with pe.Fori(0, 2) as it:
                        for r in range(4):
                            step(2 + r, n0 + 5 + 3 * r, it * 12, it * 4, False)
                    step(10, n0 + 5 + 24, 0, 0, False)
                pe.wait_ge(S["glo_done"], NJ * (i + 1))
                rows_stationary(INDEX["ffn_down", i, NJ - 1], 0, mine, False, True)

            pe.wait_ge(S["misc_init"], 1)
            pe.wait_ge(S["cond_lo"], 1)
            for g in range(ADA_PRE):
                ada(g, 0, g)
            for i in range(DEPTH):
                n = INDEX["ada", i, ADA_PRE]
                norm(2 * i, (n, n + 1))
                if MIXER[i] == "mlstm":
                    mlstm(i)
                else:
                    attention(i)
                n = INDEX["ada", i, ADA_PRE + 10]
                norm(2 * i + 1, tuple(range(n, n + 4)))
                gates(2 * i + 1)
                ffn(i)

        @block.scalar
        def _(act):
            def copy(out, in_, sem, scale=1.0):
                act.activation(out, in_, ACT.Copy, scale=scale).then_inc(S[sem], 1)

            def ada_out(n, i, g):
                a = ada_index(i, g)
                tile_used(act, n)
                if a:
                    act.wait_ge(S["mod_landed"], 16 * a)
                copy(mod_stage[0:4, :], ADA_PS[0:4, 0:256], "ada_evac")
                act.wait_ge(S["ada_evac"], a + 1)
                act.dma_start(mod_raw[4 * g:4 * g + 4, :], mod_stage[0:4, :]).then_inc(S["mod_landed"], 16)

            def ada_keep(n, g, adv, more):
                tile_used(act, n, adv)
                copy(mod_row[0:4, bass.ds(more * 256 + g * 256, 256)], ADA_PS[0:4, 0:256], "ada_evac")

            def ada_send(i):
                act.wait_ge(S["ada_evac"], ada_index(i, ADA_PRE))
                for g in range(ADA_PRE):
                    act.dma_start(mod_raw[4 * g:4 * g + 4, :], mod_row[0:4, g * 256:(g + 1) * 256]
                                  ).then_inc(S["mod_landed"], 16)

            def squares(q):
                if q == 0:
                    act.wait_ge(S["x_loaded"], 16)
                else:
                    act.wait_ge(S["x_done"], 2 * q)
                for s in range(NS):
                    act.activation(xn[:, s * D:(s + 1) * D], x[:, s * D:(s + 1) * D], ACT.Square,
                                   accum_out=ssq[:, s:s + 1]).then_inc(S["ssq_done"], 1)

            def norm(q, tiles):
                i = q // 2
                squares(q)
                if q % 2:
                    act.wait_ge(S["modb_done"], 3 * i + 2)
                for n in tiles:
                    split_hi(act, n + 1)
                    ada_out(n, i, ORDER[n][2])
                for g in range(4):
                    act.wait_ge(S["hf_done"], 4 * q + g + 1)
                    copy(H_hi[:, g * 512:(g + 1) * 512], hf[g % 2][:, :], "hhi_done")

            def gates(r):
                act.wait_ge(S["h_done"], 4 * r + 4)
                for b in range(4):
                    act.wait_ge(S["gate_mm"], 4 * r + b + 1)
                    copy(gate_bc[:, b * 512:(b + 1) * 512], MISC[:, :], "gate_evac")

            def splits(n0, count):
                if count >= 8:
                    with act.Fori(0, count // 4) as it:
                        for t in range(4):
                            split_hi(act, n0 + t + 1, it * 4)
                else:
                    for t in range(count):
                        split_hi(act, n0 + t + 1)

            def part(t, base_, it):
                return t[:, bass.ds(it * 4 * 512 + base_ * 512, 512)]

            def mlstm(i):
                j = ML_INDEX[i]
                act.dma_start(wg_raw[:, :], io["w_gate"][j]).then_inc(S["wg_landed"], 16)
                n0 = INDEX["ml_x", i, 0]

                def silu_hi(t, it):
                    act.wait_ge(S["conv_done"], 2 + 8 * j + t + 1 + it * 4)
                    act.wait_ge(S["xc_lo"], 8 * j + t + 1 + it * 4)
                    act.wait_ge(S["xcs_done"], 8 * j + t + 1 + it * 4)
                    act.activation(ow[t % 2][:, :], t1[t % 2][:, :], ACT.Silu).then_inc(S["xc_done"], 1)
                    act.wait_ge(S["xc_done"], 8 * j + t + 1 + it * 4)
                    copy(part(B_hi, t, it), ow[t % 2][:, :], "xc_hi")

                with act.Fori(0, 2) as it:
                    for t in range(4):
                        split_hi(act, n0 + t + 1, it * 4)
                        tile_used(act, n0 + t, it * 4)
                        copy(part(A_hi, t, it), UP[t % 2][:, :], "xm_hi")
                        for b in range(2):
                            w = COL["ml_conv_w"] + (3 * j + 1) * KI + 2 * t + b
                            c = COL["ml_conv_b"] + j * KI + 2 * t + b
                            act.activation(t1[t % 2][:, b * TOK:(b + 1) * TOK], UP[t % 2][:, b * TOK:(b + 1) * TOK],
                                           ACT.Identity, bias=small[:, bass.ds(it * 8 + c, 1)],
                                           scale=small[:, bass.ds(it * 8 + w, 1)]).then_inc(S["t1_done"], 1)
                        if t:
                            silu_hi(t - 1, it)
                    silu_hi(3, it)
                act.wait_ge(S["wg_landed"], 16 * (j + 1))
                copy(wg_hi[:, :], wg_raw[:, :], "wg_hi_done")
                n0 = INDEX["ml_qk", i, 0, 0]
                for g in range(4):
                    split_hi(act, n0 + 2 * g + 1)
                    if g == 0:
                        act.wait_ge(S["gates_mm"], j + 1)
                        act.activation(g16[0:16, :], MISC[0:16, 0:TOK], ACT.Identity,
                                       bias=sc("b_gate", j, rows=16)).then_inc(S["g16_done"], 1)
                        act.wait_ge(S["g16_done"], j + 1)
                        if j:
                            act.wait_ge(S["row_dve"], ROW_DVE * j)
                        for k, (t, r) in enumerate([(gI, 0), (gF, 0), (gI, 32), (gF, 32)]):
                            act.dma_start(t[r:r + 4, :], g16[4 * k:4 * k + 4, :]).then_inc(S["rows_landed"], 16)
                    if g == 1:
                        act.wait_ge(S["row_dve"], ROW_DVE * j + ROW_ABS)
                        act.activation(gA[0:36, :], gA[0:36, :], ACT.Exp, scale=-1.0).then_inc(S["row_act"], 1)
                        act.wait_ge(S["row_act"], ROW_ACT * j + 1)
                        act.activation(gA[0:36, :], gA[0:36, :], ACT.Ln, bias=1.0).then_inc(S["row_act"], 1)
                    if g == 3:
                        act.wait_ge(S["row_dve"], ROW_DVE * j + ROW_G)
                        act.activation(RBW[0:36, :], RB[0:36, T:TOK], ACT.Exp,
                                       bias=sc("m0", j, rows=36)).then_inc(S["row_act"], 1)
                    split_hi(act, n0 + 2 * g + 2)
                    tile_used(act, n0 + 2 * g + 1)
                    copy(Q[:, g * 512:(g + 1) * 512], UP[g % 2][:, :], "qk_evac", scale=DK ** -0.5)
                n0 += 8
                with act.Fori(0, 2) as it:
                    for g in range(2):
                        split_hi(act, n0 + 2 * g + 1, it * 4)
                        split_hi(act, n0 + 2 * g + 2, it * 4)
                        tile_used(act, n0 + 2 * g + 1, it * 4)
                        copy(K[:, bass.ds(it * 1024 + g * 512, 512)], UP[g % 2][:, :], "qk_evac")
                act.wait_ge(S["m_done"], 2 * (j + 1))
                for d in range(2):
                    act.dma_start(io["new_m"][0, j, d:d + 1, :].rearrange("a h -> h a"),
                                  m_out[32 * d:32 * d + MH, :]).then_inc(S["m_landed"], 16)
                for half in range(2):
                    n0 = INDEX["ml_v", i, half, 0]
                    splits(n0, 8)
                    tile_used(act, n0 + 7)
                    for c in range(2):
                        copy(v[:, half * 1024 + c * 512:half * 1024 + (c + 1) * 512], ACC[c][:, :], "v_evac_a")
                for h in range(MH):
                    head(i, j, h)
                n0 = INDEX["ml_z", i, 0]

                def z_hi(t, it):
                    act.wait_ge(S["z_mul"], 2 + 8 * j + t + 1 + it * 4)
                    copy(part(A_hi, t, it), ow[t % 2][:, :], "z_hi")

                with act.Fori(0, 2) as it:
                    for t in range(4):
                        split_hi(act, n0 + t + 1, it * 4)
                        tile_used(act, n0 + t, it * 4)
                        act.wait_ge(S["z_mul"], 8 * j + t + 1 + it * 4)
                        act.activation(t1[t % 2][:, :], UP[t % 2][:, :], ACT.Silu).then_inc(S["z_silu"], 1)
                        if t:
                            z_hi(t - 1, it)
                    z_hi(3, it)
                gates(2 * i)
                splits(INDEX["ml_down", i, 0], 8)

            def head(i, j, h):
                q = 4 * j + h
                n = INDEX["ml_C", i, h]
                split_hi(act, n)
                act.wait_ge(S["arg_done"], 2 * q + 2)
                for d in range(2):
                    for s in range(NS):
                        o = (2 * d + s) * T
                        act.activation(E[:, o:o + T], E[:, o:o + T], ACT.Exp,
                                       bias=ccol[:, 36 * s + 32 * d + h:36 * s + 32 * d + h + 1]
                                       ).then_inc(S["e_done"], 1)
                if q:
                    act.wait_ge(S["pt_done"], q)
                for d in range(2):
                    act.activation(Em[:, d * TOK:(d + 1) * TOK], UP[d][:, TOK:2 * TOK],
                                   ACT.Exp).then_inc(S["em_done"], 1)
                ada_out(n - 1, i, ORDER[n - 1][2])
                split_hi(act, n + 1)
                act.wait_ge(S["e_done"], 4 * q + 4)
                for d in range(2):
                    last = d * TOK + (T - 1 if d == 0 else 0)
                    act.activation(kw[:, d * DK:(d + 1) * DK], knat[:, h * DK:(h + 1) * DK], ACT.Identity,
                                   scale=E[:, last:last + 1]).then_inc(S["kw_done"], 1)
                act.wait_ge(S["qs2_done"], 2 * q + 1)
                copy(qs_hi[:, :], qs[:, :], "qs_hi_done")
                split_hi(act, n + 2)
                if q:
                    act.wait_ge(S["c_landed"], 32 * q)
                for e in range(4):
                    act.wait_ge(S["cn_mm"], 4 * q + e + 1)
                    copy(c_stage[:, e * DV:(e + 1) * DV], ACC[2 + e % 2][:, :], "cn_evac")
                act.wait_ge(S["cn_evac"], 4 * q + 4)
                for d in range(2):
                    act.dma_start(io["new_C"][0, j, d, h].rearrange("(c p) v -> p c v", p=P),
                                  v3(c_stage[:, d * HALF:(d + 1) * HALF], DV)).then_inc(S["c_landed"], 16)
                act.wait_ge(S["n_mm"], q + 1)
                if q:
                    act.wait_ge(S["n_landed"], 16 * q)
                copy(n_out[0:1, :], MISC[0:1, :], "n_evac")
                act.wait_ge(S["n_evac"], q + 1)
                act.dma_start(io["new_n"][0, j, :, h].rearrange("(a d) k -> a d k", a=1),
                              n_out[0:1, :].rearrange("p (d k) -> p d k", d=2)).then_inc(S["n_landed"], 16)
                ada_out(n + 1, i, ORDER[n + 1][2])

            def attention(i):
                a = i - 1
                nb = 4 if a == 0 else 8
                name = "swa" if a == 0 else "na"
                act.dma_start(cache[:, 0:2 * nb * P], io[name + "_cache"]).then_inc(S["cache_landed"], 16)
                if a == 0:
                    n0 = INDEX["q", i, 0]
                    splits(n0, 4)
                    tile_used(act, n0 + 3)
                    for c in range(2):
                        copy(qrow[:, c * 512:(c + 1) * 512], ACC[c][:, :], "row_q_a")
                    n0 = INDEX["kv", i, 0]
                    splits(n0, 2)
                    act.wait_ge(S["row_k"], 2)
                    for s in range(NS):
                        copy(vrow[:, s * 512:(s + 1) * 512].rearrange("p (h e d) -> p h e d", e=2, d=HD),
                             UP[s][:, 256:512].rearrange("p (h e d) -> p h e d", e=1, d=HD)
                             .to_broadcast([P, KV, 2, HD]), "row_v")
                else:
                    act.dma_start(bias[:, :], io["rpb"]).then_inc(S["bias_landed"], 16)
                    for c, rows in enumerate((qrow, krow, vrow)):
                        n0 = INDEX["qkv", i, c, 0]
                        splits(n0, 4)
                        tile_used(act, n0 + 3)
                        for k in range(2):
                            copy(rows[:, k * 512:(k + 1) * 512], ACC[k][:, :], "row_q_a")
                if a == 0:
                    act.wait_ge(S["row_v"], 1)
                    views = [t[:, 0:512].rearrange("p (h e d) -> p h e d", e=2, d=HD)[:, :, 0, :]
                             for t in (krow, vrow)]
                else:
                    act.wait_ge(S["row_q_a"], 8)
                    views = [t[:, 0:D].rearrange("p (h d) -> p h d", d=HD) for t in (krow, vrow)]
                for which, view in zip("kv", views):
                    act.dma_start(io[f"{name}_{which}"][0, 0].rearrange("h t d -> t h d"), view
                                  ).then_inc(S["kv_landed"], 16)
                for b in range(3 * nb // 4):
                    act.wait_ge(S["tk_mm"], 3 * a + b + 1)
                    copy(kT[:, b * 512:(b + 1) * 512], UP[b % 2][:, :], "tk_evac")
                n = INDEX["ada", i, ADA_PRE + 2]
                for u in range(8):
                    g, s = u // 2, u % 2
                    w = 8 * a + u
                    width = (1 + s) * T
                    split_hi(act, n + u + 1)
                    act.wait_ge(S["nm_done"], w + 1)
                    for k in range(4):
                        if a == 1 and s == 1:
                            src, scale = Sa[:, k * width:(k + 1) * width], 1.0
                        else:
                            src, scale = ACC[k // 2][:, (k % 2) * width:(k % 2 + 1) * width], HD ** -0.5
                        act.activation(Ea[:, k * width:(k + 1) * width], src, ACT.Exp, bias=nm[:, k:k + 1], scale=scale,
                                       accum_out=sums[:, k:k + 1]).then_inc(S["exp_done"], 1)
                    if a == 0:
                        act.wait_ge(S["esink_in"], w + 1)
                        act.activation(esink[:, :], esink[:, :], ACT.Exp).then_inc(S["esink_done"], 1)
                    ada_out(n + u, i, ORDER[n + u][2])
                    for b in range(1 + s):
                        act.wait_ge(S["pt_mm"], 3 * (w // 2) + s + b + 1)
                        copy(PTa[:, b * 512:(b + 1) * 512], ACC[2 + b][:, :], "pt_evac")
                    act.wait_ge(S["o_mm"], w + 1)
                    for e in range(2):
                        copy(out_half(H_hi, g, s, e), psum_half(e), "o_hi")
                gates(2 * i)
                splits(INDEX["o", i, 0], 4)

            def ffn(i):
                n0 = INDEX["ffn_up", i, 0]
                w0 = COL["ffn_conv_w"] + (3 * i + 1) * FB
                b0 = COL["ffn_conv_b"] + i * FB

                def taps(dst, bank, j, blk, jj, sem):
                    for b in range(2):
                        k = blk + 2 * j + b
                        act.activation(dst[:, b * TOK:(b + 1) * TOK], bank[:, b * TOK:(b + 1) * TOK], ACT.Identity,
                                       bias=small[:, bass.ds(jj * 2 + b0 + k, 1)],
                                       scale=small[:, bass.ds(jj * 2 + w0 + k, 1)]).then_inc(S[sem], 1)

                def step(j, n, adv, jj, with_ada, nxt):
                    split_hi(act, n + 1, adv)
                    tile_used(act, n, adv)
                    if NJ * i + j:
                        act.wait_ge(S["gt_done"], NJ * i + j + jj)
                    taps(tg, UP[0], j, 0, jj, "tg_done")
                    split_hi(act, n + 2, adv)
                    tile_used(act, n + 1, adv)
                    taps(tv, UP[1], j, FB // 2, jj, "tv_done")
                    act.wait_ge(S["cg_done"], NJ * i + j + 1 + jj)
                    act.activation(sg[:, :], tg[:, :], ACT.Silu).then_inc(S["sg_done"], 1)
                    if j > 0:
                        split_hi(act, n + 3, adv)
                        tile_used(act, n + 2, adv)
                    act.wait_ge(S["gt_done"], NJ * i + j + 1 + jj)
                    copy(G_hi[:, :], gt[:, :], "ghi_done")
                    if with_ada:
                        split_hi(act, n + 4, adv)
                        ada_keep(n + 3, j - 1, adv, jj)

                step(0, n0, 0, 0, False, 0)
                step(1, n0 + 2, 0, 0, i + 1 < DEPTH, 0)
                if i + 1 < DEPTH:
                    with act.Fori(0, NJ - 2) as it:
                        step(2, n0 + 6, it * 4, it, True, 0)
                else:
                    with act.Fori(0, 2) as it:
                        for r in range(4):
                            step(2 + r, n0 + 5 + 3 * r, it * 12, it * 4, False, 0)
                    step(10, n0 + 5 + 24, 0, 0, False, 0)
                split_hi(act, INDEX["ffn_down", i, NJ - 1] + 1)
                if i + 1 < DEPTH:
                    ada_send(i + 1)

            act.dma_start(small[:, :], io["small"]).then_inc(S["loads"], 16)
            act.dma_start(x[:, :], io["x"]).then_inc(S["x_loaded"], 16)
            act.dma_start(ada_b[0:96, :], io["ada_b"][0]).then_inc(S["adab_landed"], 16)
            act.wait_ge(S["loads"], 16)
            act.activation(cond[:, :], sc("cond", 0, 2 * KD), ACT.Silu).then_inc(S["cond_silu"], 1)
            act.wait_ge(S["cond_silu"], 1)
            copy(cond_parts[:, :].rearrange("p (k a s) -> p k a s", a=2, s=2)[:, :, 0, :], v3(cond[:, :], 2), "cond_hi")
            for k, name in enumerate(("z_silu", "qk_evac")):
                act.activation(credit[0:1, 4 + k:5 + k], sc("ones", rows=1), ACT.Copy).then_inc(S[name], 2)
            act.wait_ge(S["misc_init"], MISC_INIT)
            split_hi(act, 0)
            for g in range(ADA_PRE):
                split_hi(act, g + 1)
                ada_out(g, 0, g)
            for i in range(DEPTH):
                n = INDEX["ada", i, ADA_PRE]
                norm(2 * i, (n, n + 1))
                if MIXER[i] == "mlstm":
                    mlstm(i)
                else:
                    attention(i)
                n = INDEX["ada", i, ADA_PRE + 10]
                norm(2 * i + 1, tuple(range(n, n + 4)))
                gates(2 * i + 1)
                act.wait_ge(S["modb_done"], 3 * i + 3)
                if i + 1 == DEPTH:
                    act.dma_start(fw[:, :], io["final_w"]).then_inc(S["fw_landed"], 16)
                else:
                    act.dma_start(ada_b[0:96, :], io["ada_b"][i + 1]).then_inc(S["adab_landed"], 16)
                ffn(i)
            squares(2 * DEPTH)
            for s, y in enumerate(("y_prompt", "y_sample")):
                act.wait_ge(S["final_done"], s + 1)
                act.dma_start(io[y][0], xn[:, s * D:(s + 1) * D]).then_inc(S["y_landed"], 16)
            for name, count in (("y_landed", 2), ("c_landed", 16), ("n_landed", 8), ("m_landed", 4), ("kv_landed", 4)):
                act.wait_ge(S[name], 16 * count)

        @block.vector
        def _(dve):
            link = Link(dve, "dve_link")
            row = Link(dve, "row_dve")

            def add_mod(i, rows, tiles):
                dve.wait_ge(S["mod_landed"], 16 * ada_index(i, tiles))
                dve.wait_ge(S["adab_landed"], 16 * (i + 1))
                dve.tensor_tensor(mod_b[0:rows, :], mod_raw[0:rows, :], ada_b[0:rows, :],
                                  ALU.add).then_inc(S["modb_done"], 1)

            def norm(q, tiles):
                i = q // 2
                if q % 2 == 0:
                    add_mod(i, 32, ADA_PRE)
                split_lo(dve, tiles[0] + 1)
                g0 = 0 if q % 2 == 0 else SHIFT2
                ng = 8 if q % 2 == 0 else 24
                dve.wait_ge(S["modT_mm"], q + 1)
                view = modT[:, :].rearrange("p (a g r) -> p a g r", a=2, r=4)
                dve.tensor_copy(view[:, :, 0:ng, :],
                                MISC[:, 0:192].rearrange("p (a g r) -> p a g r", a=2, r=4)[:, :, 0:ng, :]
                                ).then_inc(S["modT_done"], 1)
                dve.wait_ge(S["modT_done"], q + 1)
                for coef, g in ((coef_b, g0), (coef_a, g0 + 4)):
                    for a in range(2):
                        out = coef[:, :].rearrange("p (c a s) -> p a c s", a=2, s=2)[:, a]
                        link(dve.tensor_tensor(out, view[:, a, g:g + 4, 0:2], view[:, a, g:g + 4, 2:4], ALU.add))
                link.wait()
                nw = sc("norm_w", q * KD, KD)
                link(dve.scalar_tensor_tensor(v3(coef_a[:, :], 2), v3(coef_a[:, :], 2), 1.0,
                                              nw.unsqueeze(2).to_broadcast([P, KD, 2]), ALU.add, ALU.mult))
                for n in tiles[1:]:
                    split_lo(dve, n + 1)
                dve.wait_ge(S["rstd_done"], q + 1)
                for s in range(NS):
                    dve.tensor_scalar(xn[:, s * D:(s + 1) * D], x[:, s * D:(s + 1) * D], rstd[:, s:s + 1], None,
                                      ALU.mult).then_inc(S["xn_done"], 1)
                link.wait()

                def h_lo(g):
                    dve.wait_ge(S["hhi_done"], 4 * q + g + 1)
                    dve.tensor_tensor(H_lo[:, g * 512:(g + 1) * 512], hf[g % 2][:, :],
                                      H_hi[:, g * 512:(g + 1) * 512].bitcast(F32), ALU.subtract).then_inc(S["h_done"], 1)

                for g in range(4):
                    dve.wait_ge(S["nt_done"], 4 * q + g + 1)
                    if g >= 2:
                        dve.wait_ge(S["h_done"], 4 * q + g - 1)
                    co = slice(4 * g, 4 * g + 4)
                    link(dve.tensor_tensor(v3(hf[g % 2][:, :], T), v3(ACC[g][:, :], T),
                                           coef_a[:, co].unsqueeze(2).to_broadcast([P, 4, T]), ALU.mult))
                    link.wait()
                    dve.tensor_tensor(v3(hf[g % 2][:, :], T), v3(hf[g % 2][:, :], T),
                                      coef_b[:, co].unsqueeze(2).to_broadcast([P, 4, T]),
                                      ALU.add).then_inc(S["hf_done"], 1)
                    if g:
                        h_lo(g - 1)
                h_lo(3)

            def residual(r, n):
                tile_used(dve, n)
                dve.wait_ge(S["gate_evac"], 4 * r + 4)
                tmp = t1 + ow
                for b in range(4):
                    link(dve.tensor_tensor(tmp[b][:, :], ACC[b][:, :], gate_bc[:, b * 512:(b + 1) * 512], ALU.mult))
                link.wait()
                for s in range(NS):
                    for b in (2 * s, 2 * s + 1):
                        ins = dve.tensor_tensor(x[:, b * 512:(b + 1) * 512], x[:, b * 512:(b + 1) * 512],
                                                tmp[b][:, :], ALU.add)
                    ins.then_inc(S["x_done"], 1)

            def splits(n0, count):
                if count >= 8:
                    with dve.Fori(0, count // 4) as it:
                        for t in range(4):
                            split_lo(dve, n0 + t + 1, it * 4)
                else:
                    for t in range(count):
                        split_lo(dve, n0 + t + 1)

            def side_taps(dst, bank, blk, it, per, before, after, half_sem, half_base, done_sem):
                views = []
                for b in range(2):
                    o = slice(b * TOK, (b + 1) * TOK)
                    views.append((v3(dst[:, o], T), v3(bank[:, o], T)))
                for b, (d, p) in enumerate(views):
                    dve.scalar_tensor_tensor(d[:, :, 1:T], p[:, :, 0:T - 1], small[:, bass.ds(it * per + before + blk + b, 1)],
                                             d[:, :, 1:T], ALU.mult, ALU.add).then_inc(S[half_sem], 1)
                dve.wait_ge(S[half_sem], half_base)
                for b, (d, p) in enumerate(views):
                    ins = dve.scalar_tensor_tensor(d[:, :, 0:T - 1], p[:, :, 1:T],
                                                   small[:, bass.ds(it * per + after + blk + b, 1)],
                                                   d[:, :, 0:T - 1], ALU.mult, ALU.add)
                ins.then_inc(S[done_sem], 1)

            def part(t, base_, it):
                return t[:, bass.ds(it * 4 * 512 + base_ * 512, 512)]

            def mlstm(i):
                j = ML_INDEX[i]
                n0 = INDEX["ml_x", i, 0]
                w0 = COL["ml_conv_w"] + 3 * j * KI

                def xc_lo(t, it):
                    dve.wait_ge(S["xc_hi"], 8 * j + t + 1 + it * 4)
                    dve.tensor_tensor(part(B_lo, t, it), ow[t % 2][:, :], part(B_hi, t, it).bitcast(F32),
                                      ALU.subtract).then_inc(S["xc_lo"], 1)

                with dve.Fori(0, 2) as it:
                    for t in range(4):
                        k = 8 * j + t
                        split_lo(dve, n0 + t + 1, it * 4)
                        dve.wait_ge(S["xm_hi"], k + 1 + it * 4)
                        dve.wait_ge(S["t1_done"], 2 * k + 2 + it * 8)
                        dve.tensor_tensor(part(A_lo, t, it), UP[t % 2][:, :], part(A_hi, t, it).bitcast(F32),
                                          ALU.subtract)
                        side_taps(t1[t % 2], UP[t % 2], 2 * t, it, 8, w0, w0 + 2 * KI, "conv_half",
                                  2 * k + 2 + it * 8, "conv_done")
                        if t:
                            xc_lo(t - 1, it)
                    xc_lo(3, it)
                dve.wait_ge(S["wg_hi_done"], j + 1)
                dve.tensor_tensor(wg_lo[:, :], wg_raw[:, :], wg_hi[:, :].bitcast(F32),
                                  ALU.subtract).then_inc(S["wg_done"], 1)
                n0 = INDEX["ml_qk", i, 0, 0]
                for g in range(4):
                    split_lo(dve, n0 + 2 * g + 1)
                    if g == 1:
                        dve.wait_ge(S["rows_landed"], 64 * (j + 1))
                        row(dve.scalar_tensor_tensor(gA[0:36, :], gF[0:36, :], -1.0, gF[0:36, :], ALU.mult, ALU.max))
                        row(dve.tensor_scalar(gM[0:36, :], gF[0:36, :], 0.0, None, ALU.min))
                    if g == 2:
                        dve.wait_ge(S["row_act"], ROW_ACT * j + 2)
                        row.wait()
                        row(dve.tensor_tensor(gM[0:36, :], gM[0:36, :], gA[0:36, :], ALU.subtract))
                        row.wait()

                        def scan(dst, src, add, op, initial):
                            for r0, step in ((0, 1), (32, -1)):
                                for s in range(NS):
                                    o = slice(s * T, (s + 1) * T)
                                    rows = slice(r0, r0 + MH)
                                    other = gz[rows, 0:T] if add else src[rows, o][:, ::step]
                                    init = initial(r0, s)
                                    row(dve.tensor_tensor_scan(dst[rows, o][:, ::step], src[rows, o][:, ::step],
                                                               other, init, op, op))
                            row.wait()

                        scan(gb, gM, True, ALU.add, lambda r0, s: 0.0)
                        row(dve.tensor_tensor(gc[0:36, :], gI[0:36, :], gb[0:36, :], ALU.subtract))
                        row.wait()
                        scan(gG, gc, False, ALU.max,
                             lambda r0, s: sc("m0", j, rows=MH, r0=r0) if s else 0.0)
                        row(dve.tensor_scalar(RB[0:36, 0:TOK], gG[0:36, :], -1.0, None, ALU.mult))
                        row(dve.scalar_tensor_tensor(RB[0:36, TOK:2 * TOK], gb[0:36, :], -1.0, gG[0:36, :],
                                                     ALU.mult, ALU.subtract))
                        row.wait()
                        if j:
                            dve.wait_ge(S["m_landed"], 32)
                        for r0, last in ((0, TOK + T - 1), (32, TOK)):
                            dve.tensor_scalar(m_out[r0:r0 + MH, :], RB[r0:r0 + MH, last:last + 1], -1.0, None,
                                              ALU.mult).then_inc(S["m_done"], 1)
                    split_lo(dve, n0 + 2 * g + 2)
                splits(n0 + 8, 8)
                for b in range(4):
                    dve.wait_ge(S["st_mm"], 4 * j + b + 1)
                    dst = (ST, knat)[b // 2]
                    dve.tensor_copy(dst[:, (b % 2) * 512:(b % 2 + 1) * 512], ACC[b][:, :]).then_inc(S["st_evac"], 1)
                dve.wait_ge(S["c_mm"], j + 1)
                row(dve.tensor_copy(ccol[:, :], MISC[:, 0:72]))
                assert row.n == ROW_DVE * (j + 1)
                for half in range(2):
                    n0 = INDEX["ml_v", i, half, 0]
                    splits(n0, 8)
                    tile_used(dve, n0 + 7)
                    for c in range(2):
                        o = DIN + half * 1024 + c * 512
                        dve.tensor_copy(v[:, o:o + 512], ACC[2 + c][:, :]).then_inc(S["v_evac_d"], 1)
                dve.wait_ge(S["xcs_done"], 2 + 8 * (j + 1))
                dve.wait_ge(S["st_evac"], 4 * (j + 1))
                for h in range(MH):
                    head(i, j, h)
                add_mod(i, 96, 20)
                n0 = INDEX["ml_z", i, 0]

                def z_lo(t, it):
                    dve.wait_ge(S["z_hi"], 8 * j + t + 1 + it * 4)
                    dve.tensor_tensor(part(A_lo, t, it), ow[t % 2][:, :], part(A_hi, t, it).bitcast(F32),
                                      ALU.subtract).then_inc(S["z_lo"], 1)

                dve.wait_ge(S["hc_done"], 4 * (j + 1))
                with dve.Fori(0, 2) as it:
                    for t in range(4):
                        split_lo(dve, n0 + t + 1, it * 4)
                        dve.wait_ge(S["z_lo"], 8 * j + t + 1 + it * 4)
                        dve.wait_ge(S["z_silu"], 2 + 8 * j + t + 1 + it * 4)
                        dve.tensor_tensor(ow[t % 2][:, :], part(XCS, t, it), t1[t % 2][:, :],
                                          ALU.mult).then_inc(S["z_mul"], 1)
                        if t:
                            z_lo(t - 1, it)
                    z_lo(3, it)
                n0 = INDEX["ml_down", i, 0]
                splits(n0, 8)
                residual(2 * i, n0 + 7)

            def head(i, j, h):
                q = 4 * j + h
                n = INDEX["ml_C", i, h]
                split_lo(dve, n)
                dve.wait_ge(S["bc_mm"], q + 1)
                for d, mask in enumerate(("mask_f", "mask_b")):
                    dve.tensor_tensor(v3(E[:, d * TOK:(d + 1) * TOK], T), v3(UP[d][:, 0:TOK], T),
                                      sc(mask, 0, T).unsqueeze(1).to_broadcast([P, NS, T]),
                                      ALU.add).then_inc(S["arg_done"], 1)
                four = lambda ap: ap.rearrange("p (d c t) -> p d c t", d=2, c=2)
                for d in range(2):
                    qv = Q[:, 2 * h * TOK:(2 * h + 2) * TOK].rearrange("p (c s t) -> p c s t", c=2, s=2)[:, :, 1, :]
                    ins = dve.tensor_tensor(four(qs[:, :])[:, d], qv,
                                            ACC[0][:, d * T:(d + 1) * T].unsqueeze(1).to_broadcast([P, 2, T]), ALU.mult)
                ins.then_inc(S["qs_done"], 1)
                split_lo(dve, n + 1)
                dve.wait_ge(S["e_done"], 4 * q + 4)
                for d in range(2):
                    ins = dve.tensor_tensor(Pw[:, d * TOK:(d + 1) * TOK], E[:, d * TOK:(d + 1) * TOK],
                                            ST[:, h * TOK:(h + 1) * TOK], ALU.mult)
                ins.then_inc(S["p_done"], 1)
                dve.wait_ge(S["den_mm"], q + 1)
                dve.wait_ge(S["em_done"], 2 * q + 2)
                link(dve.scalar_tensor_tensor(den[:, :], ACC[1][:, :], -1.0, Em[:, :], ALU.mult, ALU.max))
                link.wait()
                link(dve.tensor_tensor(den[:, :], ACC[1][:, :], den[:, :], ALU.max))
                link.wait()
                link(dve.reciprocal(den[:, :], den[:, :]))
                link.wait()
                for d in range(2):
                    ins = dve.tensor_tensor(four(qs[:, :])[:, d], four(qs[:, :])[:, d],
                                            den[:, d * TOK + T:(d + 1) * TOK].unsqueeze(1).to_broadcast([P, 2, T]),
                                            ALU.mult)
                ins.then_inc(S["qs2_done"], 1)
                link(dve.tensor_tensor(Pw[:, :], Pw[:, :], den[:, :], ALU.mult))
                link.wait()
                dve.tensor_tensor(PT[:, :], Pw[:, 0:TOK], Pw[:, TOK:2 * TOK], ALU.add).then_inc(S["pt_done"], 1)
                dve.wait_ge(S["qs_hi_done"], q + 1)
                dve.tensor_tensor(qs_lo[:, :], qs[:, :], qs_hi[:, :].bitcast(F32),
                                  ALU.subtract).then_inc(S["qs2_done"], 1)
                split_lo(dve, n + 2)
                tile_used(dve, n)
                for s in range(NS):
                    link(dve.bn_stats(bn[:, 6 * s:6 * s + 6], ACC[s][:, :]))
                link.wait()
                for s in range(NS):
                    ins = dve.bn_aggr(mv[:, 2 * s:2 * s + 2], bn[:, 6 * s:6 * s + 6])
                ins.then_inc(S["var_done"], 1)
                dve.wait_ge(S["rstd2_done"], q + 1)
                dve.wait_ge(S["var_done"], q + 1)
                for s in range(NS):
                    dve.tensor_scalar(hn[:, s * DV:(s + 1) * DV], ACC[s][:, :], mv[:, 2 * s:2 * s + 1],
                                      rstd[:, s:s + 1], ALU.subtract, ALU.mult).then_inc(S["hn_done"], 1)
                dve.wait_ge(S["ht_mm"], q + 1)
                for f in range(4):
                    k = 4 * h + f
                    o = slice(k * TOK, (k + 1) * TOK)
                    ins = dve.scalar_tensor_tensor(XCS[:, o], UP[f // 2][:, (f % 2) * TOK:(f % 2 + 1) * TOK],
                                                   sc("ml_norm_w", j * KI + k), XCS[:, o], ALU.mult, ALU.add)
                ins.then_inc(S["hc_done"], 1)

            def rope(t, c0, heads, own):
                own.wait()
                if c0 != D:
                    dve.wait_ge(S["roped"], 1)
                w = heads * HD
                xv, uv = (ap.rearrange("p (h f e w) -> p h f e w", f=2, e=2, w=16)
                          for ap in (t[:, c0:c0 + w], rope_u[:, 0:w]))
                tab = sc("sin", 0, 64).rearrange("p (f e w) -> p f e w", f=2, e=2)
                for f in range(2):
                    for e in range(2):
                        link(dve.tensor_tensor(uv[:, :, f, e, :], xv[:, :, f, 1 - e, :],
                                               tab[:, f, e, :].unsqueeze(1).to_broadcast([P, heads, 16]), ALU.mult))
                link(dve.tensor_tensor(v3(rope_t[:, 0:w], HD), v3(t[:, c0:c0 + w], HD),
                                       sc("cos", 0, 64).unsqueeze(1).to_broadcast([P, heads, HD]), ALU.mult))
                link.wait()
                dve.tensor_tensor(t[:, c0:c0 + w], rope_t[:, 0:w], rope_u[:, 0:w], ALU.add).then_inc(S["roped"], 1)

            def attention(i):
                a = i - 1
                if a == 0:
                    n0 = INDEX["q", i, 0]
                    splits(n0, 4)
                    tile_used(dve, n0 + 3)
                    rows_q = Link(dve, "row_q_d")
                    for c in range(2):
                        rows_q(dve.tensor_copy(qrow[:, D + c * 512:D + (c + 1) * 512], ACC[2 + c][:, :]))
                    n0 = INDEX["kv", i, 0]
                    splits(n0, 1)
                    rope(qrow, D, NH, rows_q)
                    splits(n0 + 1, 1)
                    tile_used(dve, n0 + 1)
                    rows_k = Link(dve, "row_k")
                    for s in range(NS):
                        rows_k(dve.tensor_copy(
                            krow[:, s * 512:(s + 1) * 512].rearrange("p (h e d) -> p h e d", e=2, d=HD),
                            UP[s][:, 0:256].rearrange("p (h e d) -> p h e d", e=1, d=HD)
                            .to_broadcast([P, KV, 2, HD])))
                    rope(krow, 512, 2 * KV, rows_k)
                    link(dve.tensor_scalar(nsink[:, :], sc("sink", 0, NH), -1.0, None, ALU.mult))
                else:
                    for c, rows in enumerate((qrow, krow, vrow)):
                        n0 = INDEX["qkv", i, c, 0]
                        splits(n0, 4)
                        tile_used(dve, n0 + 3)
                        for k in range(2):
                            dve.tensor_copy(rows[:, D + k * 512:D + (k + 1) * 512], ACC[2 + k][:, :]
                                            ).then_inc(S["row_q_d"], 1)
                    dve.wait_ge(S["bias_landed"], 16)
                    link(dve.tensor_tensor(v3(bias[:, :], T), v3(bias[:, :], T),
                                           sc("na_mask", 0, T).unsqueeze(1).to_broadcast([P, NH, T]), ALU.add))
                for b in range(4):
                    dve.wait_ge(S["tq_mm"], 4 * a + b + 1)
                    dve.tensor_copy(qT[:, b * 512:(b + 1) * 512], ACC[b][:, :]).then_inc(S["tq_evac"], 1)
                n = INDEX["ada", i, ADA_PRE + 2]
                for u in range(8):
                    g, s = u // 2, u % 2
                    w = 8 * a + u
                    width = (1 + s) * T
                    split_lo(dve, n + u + 1)
                    dve.wait_ge(S["s_mm"], w + 1)
                    if w:
                        dve.wait_ge(S["exp_done"], 4 * w)
                    if s == 0 or a == 0:
                        for b in range(2):
                            link(dve.tensor_reduce(mx[:, 2 * b:2 * b + 2], v3(ACC[b][:, 0:2 * width], width), AX_X,
                                                   ALU.max))
                    else:
                        for b in range(2):
                            sa, sp_ = v3(Sa[:, b * 512:(b + 1) * 512], TOK), v3(ACC[b][:, :], TOK)
                            hd = 4 * g + 2 * b
                            link(dve.scalar_tensor_tensor(sa[:, :, 0:T], sp_[:, :, 0:T], HD ** -0.5,
                                                          v3(bias[:, hd * T:(hd + 2) * T], T), ALU.mult, ALU.add))
                            link(dve.tensor_scalar(sa[:, :, T:TOK], sp_[:, :, T:TOK], HD ** -0.5, None, ALU.mult))
                        link.wait()
                        link(dve.tensor_reduce(mx[:, :], v3(Sa[:, :], TOK), AX_X, ALU.max))
                    link.wait()
                    if a == 0:
                        dve.scalar_tensor_tensor(nm[:, :], mx[:, :], -HD ** -0.5, nsink[:, 4 * g:4 * g + 4], ALU.mult,
                                                 ALU.min).then_inc(S["nm_done"], 1)
                        dve.wait_ge(S["nm_done"], w + 1)
                        dve.tensor_tensor(esink[:, :], nm[:, :], nsink[:, 4 * g:4 * g + 4],
                                          ALU.subtract).then_inc(S["esink_in"], 1)
                    else:
                        dve.tensor_scalar(nm[:, :], mx[:, :], -1.0 if s else -HD ** -0.5, None,
                                          ALU.mult).then_inc(S["nm_done"], 1)
                    dve.wait_ge(S["exp_done"], 4 * w + 4)
                    if a == 0:
                        dve.wait_ge(S["esink_done"], w + 1)
                        link(dve.tensor_tensor(sums[:, :], sums[:, :], esink[:, :], ALU.add))
                        link.wait()
                    link(dve.reciprocal(rsum[:, :], sums[:, :]))
                    link.wait()
                    ev = v3(Ea[:, 0:4 * width], width)
                    dve.tensor_tensor(ev, ev, rsum[:, :].unsqueeze(2).to_broadcast([P, 4, width]),
                                      ALU.mult).then_inc(S["pn_done"], 1)
                    dve.wait_ge(S["o_hi"], 2 * w + 2)
                    for e in range(2):
                        dve.tensor_tensor(out_half(H_lo, g, s, e), psum_half(e), out_half(H_hi, g, s, e).bitcast(F32),
                                          ALU.subtract).then_inc(S["o_lo"], 1)
                add_mod(i, 96, 20)
                n0 = INDEX["o", i, 0]
                splits(n0, 4)
                residual(2 * i, n0 + 3)

            def ffn(i):
                n0 = INDEX["ffn_up", i, 0]
                w0 = COL["ffn_conv_w"] + 3 * i * FB

                def step(j, n, adv, jj, with_ada):
                    k = NJ * i + j
                    split_lo(dve, n + 1, adv)
                    dve.wait_ge(S["tg_done"], 2 * k + 2 + jj * 2)
                    side_taps(tg, UP[0], 2 * j, jj, 2, w0, w0 + 2 * FB, "cg_half", 2 * k + 2 + jj * 2, "cg_done")
                    split_lo(dve, n + 2, adv)
                    dve.wait_ge(S["tv_done"], 2 * k + 2 + jj * 2)
                    side_taps(tv, UP[1], FB // 2 + 2 * j, jj, 2, w0, w0 + 2 * FB, "cv_half", 2 * k + 2 + jj * 2,
                              "cv_done")
                    if j > 0:
                        split_lo(dve, n + 3, adv)
                    dve.wait_ge(S["ghi_done"], k + 1 + jj)
                    dve.tensor_tensor(G_lo[:, :], gt[:, :], G_hi[:, :].bitcast(F32),
                                      ALU.subtract).then_inc(S["glo_done"], 1)
                    if with_ada:
                        split_lo(dve, n + 4, adv)

                step(0, n0, 0, 0, False)
                step(1, n0 + 2, 0, 0, i + 1 < DEPTH)
                if i + 1 < DEPTH:
                    with dve.Fori(0, NJ - 2) as it:
                        step(2, n0 + 6, it * 4, it, True)
                else:
                    with dve.Fori(0, 2) as it:
                        for r in range(4):
                            step(2 + r, n0 + 5 + 3 * r, it * 12, it * 4, False)
                    step(10, n0 + 5 + 24, 0, 0, False)
                split_lo(dve, INDEX["ffn_down", i, NJ - 1] + 1)
                residual(2 * i + 1, INDEX["ffn_down", i, NJ - 1])

            for k, name in enumerate(("conv_done", "xc_lo", "z_mul", "z_lo")):
                dve.memset(credit[0:1, k:k + 1], 0.0).then_inc(S[name], 2)
            dve.wait_ge(S["misc_init"], MISC_INIT)
            dve.wait_ge(S["cond_hi"], 1)
            parts = cond_parts[:, :].rearrange("p (k a s) -> p k a s", a=2, s=2)
            dve.tensor_tensor(parts[:, :, 1, :], v3(cond[:, :], 2), parts[:, :, 0, :].bitcast(F32),
                              ALU.subtract).then_inc(S["cond_lo"], 1)
            split_lo(dve, 0)
            for g in range(ADA_PRE):
                split_lo(dve, g + 1)
            for i in range(DEPTH):
                n = INDEX["ada", i, ADA_PRE]
                norm(2 * i, (n, n + 1))
                if MIXER[i] == "mlstm":
                    mlstm(i)
                else:
                    attention(i)
                n = INDEX["ada", i, ADA_PRE + 10]
                norm(2 * i + 1, tuple(range(n, n + 4)))
                add_mod(i, 96, 24)
                ffn(i)
            dve.wait_ge(S["rstd_done"], 2 * DEPTH + 1)
            dve.wait_ge(S["fw_landed"], 16)
            for s in range(NS):
                o = slice(s * D, (s + 1) * D)
                dve.scalar_tensor_tensor(xn[:, o], x[:, o], rstd[:, s:s + 1], fw[:, :], ALU.mult,
                                         ALU.mult).then_inc(S["final_done"], 1)

        @block.gpsimd
        def _(pool):
            chain = Link(pool, "pool_chain")
            zeroed = [gI, gF, gA, gM, gb, gc, gG, RB, RBW, gz, mod_raw, mod_b]
            for t in zeroed:
                pool.memset(t[:, :], 0.0).then_inc(S["misc_init"], 1)
            pool.memset(half_pow[:, :], -0.5).then_inc(S["misc_init"], 1)
            assert len(zeroed) + 1 == MISC_INIT
            pool.memset(credit[0:1, 6:7], 0.0).then_inc(S["xcs_done"], 2)
            pool.wait_ge(S["misc_init"], MISC_INIT)
            pool.wait_ge(S["loads"], 16)

            def inverse_root(src, scale, done):
                if chain.n:
                    chain.wait()
                chain(pool.tensor_scalar(var[:, :], src, scale, EPS, ALU.mult, ALU.add))
                chain.wait()
                pool.tensor_tensor(rstd[:, :], var[:, :], half_pow[:, :], ALU.pow).then_inc(S[done], 1)

            def norm(q):
                pool.wait_ge(S["ssq_done"], 2 * q + 2)
                inverse_root(ssq[:, :], 1.0 / D, "rstd_done")

            for i in range(DEPTH):
                norm(2 * i)
                if MIXER[i] == "mlstm":
                    j = ML_INDEX[i]
                    with pool.Fori(0, 2) as it:
                        for t in range(4):
                            pool.wait_ge(S["xc_done"], 8 * j + t + 1 + it * 4)
                            skip = small[:, bass.ds(it * 8 + COL["ml_skip"] + j * KI + 2 * t, 2)]
                            pool.tensor_tensor(v3(XCS[:, bass.ds(it * 2048 + t * 512, 512)], TOK), v3(ow[t % 2][:, :], TOK),
                                               skip.unsqueeze(2).to_broadcast([P, 2, TOK]),
                                               ALU.mult).then_inc(S["xcs_done"], 1)
                    for h in range(MH):
                        q = 4 * j + h
                        pool.wait_ge(S["var_done"], q + 1)
                        if q:
                            pool.wait_ge(S["hn_done"], 2 * q)
                        inverse_root(v3(mv[:, :], 2)[:, :, 1], 1.0, "rstd2_done")
                norm(2 * i + 1)

                def gated(k, kk):
                    pool.wait_ge(S["sg_done"], k + 1 + kk)
                    pool.wait_ge(S["cv_done"], k + 1 + kk)
                    if k:
                        pool.wait_ge(S["glo_done"], k + kk)
                    pool.tensor_tensor(gt[:, :], sg[:, :], tv[:, :], ALU.mult).then_inc(S["gt_done"], 1)

                gated(NJ * i, 0)
                with pool.Fori(0, NJ - 1) as it:
                    gated(NJ * i + 1, it)
            norm(2 * DEPTH)


ROW_ABS, ROW_C, ROW_G, ROW_DVE = 1, 8, 13, 15
ROW_ACT = 3
MISC_INIT = 13


def kernel(**inputs):
    import concourse.bacc as bacc
    from concourse.bass_utils import run_bass_kernel_spmd

    nc = bacc.Bacc("TRN2", target_bir_lowering=False, num_devices=1, dynamic_dma_scratch_size=1024)
    arrays = {f"in_{k}": np.ascontiguousarray(a) for k, a in
              host_arrays({k: np.asarray(a) for k, a in inputs.items()}).items()}
    io = {}
    for k, a in arrays.items():
        io[k[3:]] = nc.dram_tensor(k, a.shape, F32, kind="ExternalInput").ap()
    for name, shape in OUTPUTS:
        io[name] = nc.dram_tensor(f"out_{name}", shape, F32, kind="ExternalOutput").ap()
    build(nc, io)
    r = run_bass_kernel_spmd(nc, [arrays], core_ids=[0])
    return tuple(r.results[0][f"out_{name}"] for name, _ in OUTPUTS)
```

```python
import numpy as np
import concourse.bass as bass
import concourse.mybir as mybir

F32 = mybir.dt.float32
F32R = mybir.dt.float32r
ALU = mybir.AluOpType
ACT = mybir.ActivationFunctionType
AX_X = mybir.AxisListType.X

P = 128
D = 1024
DEPTH = 4
T = 128
NS = 2
TOK = NS * T
KD = D // P
DFF = 2816
FB = 2 * DFF // P
NJ = DFF // 256
DIN = 2 * D
KI = DIN // P
MH = 4
DK = DIN // (2 * MH)
DV = DIN // MH
HD = 64
NH = D // HD
KV = NH // 4
EPS = 1e-6
NEG = -1e30

TILE = 2048
HALF = TILE // 2
RAW = 4
SPL = 4
MIXER = ["mlstm", "swa", "na", "mlstm"]
ML_INDEX = {0: 0, 3: 1}
ADA_TILES = 24
ADA_PHASE = 8
SHIFT1, SCALE1, GATE1, SHIFT2, SCALE2, GATE2 = ((32 * (p // 2), 256 * (p % 2)) for p in range(6))
MOD_ROWS = 80
ADA_M = 68
ADA_W = 16 + ADA_M

_SMALL = [("ident", 128), ("mask_f", 128), ("mask_b", 128), ("na_mask", 128), ("ones", 1), ("cos", 64),
          ("sin", 64), ("ffn_conv_w", DEPTH * 3 * FB), ("ffn_conv_b", DEPTH * FB), ("norm_w", DEPTH * 2 * KD),
          ("ml_conv_w", 2 * 3 * KI), ("ml_conv_b", 2 * KI), ("ml_norm_w", 2 * KI), ("ml_skip", 2 * KI),
          ("n0", 2 * 16), ("m0", 2), ("b_gate", 2), ("gate_sel", 8), ("sink", NH), ("cond", 2 * KD)]
COL = {}
_at = 0
for _name, _n in _SMALL:
    COL[_name] = _at
    _at += _n
NSMALL = _at


def stream_order():
    order = [("ada", 0, g) for g in range(ADA_PHASE)]
    for i in range(DEPTH):
        ada = [("ada", i, g) for g in range(ADA_PHASE, ADA_TILES)]
        if MIXER[i] == "mlstm":
            order += [("ml_x", i, t) for t in range(8)]
            order += [("ml_qk", i, g, k) for g in range(8) for k in range(2)]
            order += [("ml_v", i, c, t) for c in range(2) for t in range(8)]
            for h in range(MH):
                order += ada[4 * h:4 * h + 2] + [("ml_C", i, h)] + ada[4 * h + 2:4 * h + 4]
            order += [("ml_z", i, t) for t in range(8)]
            order += [("ml_down", i, t) for t in range(8)]
        elif MIXER[i] == "swa":
            order += [("q", i, t) for t in range(4)] + [("kv", i, t) for t in range(2)]
            order += ada
            order += [("o", i, t) for t in range(4)]
        else:
            order += [("qkv", i, c, t) for c in range(3) for t in range(4)]
            order += ada
            order += [("o", i, t) for t in range(4)]
        order += [("ffn_up", i, 0), ("ffn_up", i, NJ)]
        for j in range(1, NJ):
            order += [("ffn_up", i, j), ("ffn_up", i, NJ + j), ("ffn_down", i, j - 1)]
            if i + 1 < DEPTH and 2 <= j < 2 + ADA_PHASE:
                order += [("ada", i + 1, j - 2)]
        order += [("ffn_down", i, NJ - 1)]
    return order


ORDER = stream_order()
NT = len(ORDER)
INDEX = {tile: n for n, tile in enumerate(ORDER)}


def chunked(w, k0, nk, c0, nc):
    return w[k0 * P:(k0 + nk) * P, c0:c0 + nc].reshape(nk, P, nc).transpose(1, 0, 2).reshape(P, nk * nc)


def host_tile(tile, w):
    kind, i = tile[0], tile[1]
    j = ML_INDEX.get(i, 0)
    if kind == "ada":
        return chunked(w["ada_w"][i], 0, 8, 256 * tile[2], 256)
    if kind == "ml_x":
        return chunked(w["ml_w_up"][j], 0, 8, 256 * tile[2], 256)
    if kind == "ml_z":
        return chunked(w["ml_w_up"][j], 0, 8, DIN + 256 * tile[2], 256)
    if kind == "ml_qk":
        return chunked(w["ml_w_qk"][j], 8 * tile[3], 8, 256 * tile[2], 256)
    if kind == "ml_v":
        return chunked(w["ml_w_v"][j], 2 * tile[3], 2, 1024 * tile[2], 1024)
    if kind == "ml_C":
        c = w["state_mlstm_C"][0, j, :, tile[2]]
        return c.reshape(2, 2, P, DV).transpose(2, 0, 1, 3).reshape(P, TILE)
    if kind == "ml_down":
        return chunked(w["ml_w_down"][j], 2 * tile[2], 2, 0, 1024)
    if kind == "q":
        return chunked(w["swa_w_qkv"][0], 2 * tile[2], 2, 0, 1024)
    if kind == "kv":
        return chunked(w["swa_w_qkv"][0], 4 * tile[2], 4, 1024, 512)
    if kind == "qkv":
        return chunked(w["na_w_qkv"][0], 2 * tile[3], 2, 1024 * tile[2], 1024)
    if kind == "o":
        return chunked(w["swa_w_o" if MIXER[i] == "swa" else "na_w_o"][0], 2 * tile[2], 2, 0, 1024)
    if kind == "ffn_up":
        return chunked(w["ffn_w_up"][i], 0, 8, 256 * tile[2], 256)
    return chunked(w["ffn_w_down"][i], 2 * tile[2], 2, 0, 1024)


HEAD_ORDER = [4 * g + p // 2 + 2 * (p % 2) for g in range(NH // 4) for p in range(4)]


def columns(v):
    return np.asarray(v).reshape(-1, P).T


def host_arrays(w):
    f = np.float32
    stream = np.empty((NT, P, TILE), f)
    for n, tile in enumerate(ORDER):
        stream[n] = host_tile(tile, w)
    small = np.zeros((P, NSMALL), f)

    def put(name, a, rows=P):
        a = np.asarray(a, f)
        small[:rows, COL[name]:COL[name] + a.shape[1]] = a

    r = np.arange(P)
    put("ident", np.eye(P))
    put("mask_f", np.where(r[:, None] <= r[None, :], 0.0, NEG))
    put("mask_b", np.where(r[:, None] >= r[None, :], 0.0, NEG))
    col = r % 64
    start = np.clip(col - 8, 0, 64 - 16)
    ok = (col[None, :] >= start[:, None]) & (col[None, :] < start[:, None] + 16)
    put("na_mask", np.where(ok, 0.0, NEG))
    put("ones", np.ones((P, 1)))
    inv = np.power(f(10000.0), -np.arange(16, dtype=f) / f(16))
    ang = np.stack([(r // 64).astype(f)[:, None] * inv, col.astype(f)[:, None] * inv], 1)
    cos, sin = np.cos(ang), np.sin(ang)
    put("cos", np.stack([cos, cos], 2).reshape(P, 64))
    put("sin", np.stack([-sin, sin], 2).reshape(P, 64))
    put("ffn_conv_w", columns(w["ffn_conv_w"]))
    put("ffn_conv_b", columns(w["ffn_conv_b"]))
    put("norm_w", columns(w["norm_w"]))
    put("ml_conv_w", columns(w["ml_conv_w"]))
    put("ml_conv_b", columns(w["ml_conv_b"]))
    put("ml_norm_w", columns(w["ml_norm_w"]))
    put("ml_skip", columns(w["ml_skip"]))
    put("n0", columns(w["state_mlstm_n"][0]))
    for j in range(2):
        small[0:MH, COL["m0"] + j] = w["state_mlstm_m"][0, j, 0]
        small[32:32 + MH, COL["m0"] + j] = w["state_mlstm_m"][0, j, 1]
        small[0:16, COL["b_gate"] + j] = w["ml_b_gate"][j]
    sel = np.zeros((MOD_ROWS, 8))
    for base in (0, 32, 64):
        for g in range(4):
            for s in range(NS):
                sel[base + 4 * g + s, 2 * g + s] = sel[base + 4 * g + 2 + s, 2 * g + s] = 1.0
    put("gate_sel", sel, MOD_ROWS)
    put("sink", np.broadcast_to(w["swa_sink"][0][HEAD_ORDER], (P, NH)))
    put("cond", np.stack([columns(w["c_ctx"]), columns(w["c"][0])], 2).reshape(P, 2 * KD))
    ada_b = np.zeros((DEPTH, MOD_ROWS, 2, 256), f)
    for p in range(6):
        row = 32 * (p // 2)
        for g in range(4):
            ada_b[:, row + 4 * g:row + 4 * g + 2, p % 2] = w["ada_b"].reshape(DEPTH, 6, 4, 1, 256)[:, p, g]
    dq = np.arange(T)
    dr = (dq // 64)[None, :] - (dq // 64)[:, None] + 7
    dc = np.clip((dq % 64)[None, :] - (dq % 64)[:, None], -15, 15) + 15
    rpb = w["na_rpb"][0][HEAD_ORDER][:, dr, dc]
    return {
        "stream": stream, "small": small,
        "x": np.concatenate([w["x_prompt"][0], w["x_sample"][0]], 1),
        "ada_b": ada_b.reshape(DEPTH, MOD_ROWS, 512),
        "w_gate": np.stack([chunked(w["ml_w_gate"][j], 0, KI, 0, 16) for j in range(2)]),
        "rpb": np.ascontiguousarray(rpb.transpose(1, 0, 2)).reshape(T, NH * T),
        "final_w": np.broadcast_to(w["final_norm_w"], (P, D)),
        "swa_cache": np.concatenate([np.repeat(w[n][0, 0].transpose(1, 0, 2), 2, axis=1).reshape(T, 2 * KV * HD)
                                     for n in ("cache_swa_k", "cache_swa_v")], 1),
        "na_cache": np.concatenate([w["cache_na_k"][0, 0].transpose(1, 0, 2).reshape(T, D),
                                    w["cache_na_v"][0, 0].transpose(1, 0, 2).reshape(T, D)], 1),
    }


OUTPUTS = [("y_prompt", (1, T, D)), ("y_sample", (1, T, D)), ("new_C", (1, 2, 2, MH, DK, DV)),
           ("new_n", (1, 2, 2, MH, DK)), ("new_m", (1, 2, 2, MH)),
           ("swa_k", (1, 1, KV, T, HD)), ("swa_v", (1, 1, KV, T, HD)),
           ("na_k", (1, 1, NH, T, HD)), ("na_v", (1, 1, NH, T, HD))]


def build(nc, io):
    base = (nc.sbuf_base + 63) // 64 * 64
    KB = 1024

    def sb(name, cols, dt, at, rows=P):
        return nc.alloc_sbuf_tensor_at(name, [rows, cols], dt, offset=base + at)

    raw = [sb(f"raw{r}", TILE, F32, 8 * KB * r) for r in range(RAW)]
    spl_hi = [sb(f"spl_hi{r}", HALF, F32R, 32 * KB + 4 * KB * r) for r in range(SPL)]
    spl_lo = [sb(f"spl_lo{r}", HALF, F32R, 48 * KB + 4 * KB * r) for r in range(SPL)]
    x = sb("x", NS * D, F32, 64 * KB)
    H_hi = sb("H_hi", KD * TOK, F32R, 72 * KB)
    H_lo = sb("H_lo", KD * TOK, F32R, 80 * KB)
    rA, rB, rX, rT, rW = 88 * KB, 120 * KB, 152 * KB, 168 * KB, 184 * KB
    A_hi = sb("A_hi", KI * TOK, F32R, rA)
    A_lo = sb("A_lo", KI * TOK, F32R, rA + 16 * KB)
    B_hi = sb("B_hi", KI * TOK, F32R, rB)
    B_lo = sb("B_lo", KI * TOK, F32R, rB + 16 * KB)
    XCS = sb("XCS", KI * TOK, F32, rX)
    v = sb("v", NS * DIN, F32, rB)
    ST = sb("ST", MH * TOK, F32, rB + 16 * KB)
    knat = sb("knat", D, F32, rB + 20 * KB)
    c_stage = sb("c_stage", TILE, F32, rB + 24 * KB)
    E = sb("E", 2 * TOK, F32, rA)
    Pw = sb("Pw", 2 * TOK, F32, rA + 2 * KB)
    Em = sb("Em", 2 * TOK, F32, rA + 4 * KB)
    den = sb("den", 2 * TOK, F32, rA + 6 * KB)
    PT = sb("PT", TOK, F32, rA + 8 * KB)
    qs = sb("qs", 4 * T, F32, rA + 9 * KB)
    qs_hi = sb("qs_hi", 4 * T, F32R, rA + 11 * KB)
    qs_lo = sb("qs_lo", 4 * T, F32R, rA + 13 * KB)
    hn = sb("hn", NS * DV, F32, rA + 15 * KB)
    kw = sb("kw", 2 * DK, F32, rA + 19 * KB)
    xn = sb("xn", NS * D, F32, rT)
    hf = [sb(f"hf{b}", 2 * TOK, F32, rT + 8 * KB + 2 * KB * b) for b in range(2)]
    wg_raw = sb("wg_raw", KI * 16, F32, rT)
    wg_hi = sb("wg_hi", KI * 16, F32R, rT + 1 * KB)
    wg_lo = sb("wg_lo", KI * 16, F32R, rT + 2 * KB)
    Q = sb("Q", KD * TOK, F32, rT)
    K = sb("K", KD * TOK, F32, rT + 8 * KB)
    gate_bc = sb("gate_bc", NS * D, F32, rT + 8 * KB)
    t1 = [sb(f"t1_{b}", 2 * TOK, F32, rW + 2 * KB * b) for b in range(2)]
    ow = [sb(f"ow{b}", 2 * TOK, F32, rW + 4 * KB + 2 * KB * b) for b in range(2)]
    tg = sb("tg", 2 * TOK, F32, rX)
    tv = sb("tv", 2 * TOK, F32, rX + 2 * KB)
    sg = sb("sg", 2 * TOK, F32, rX + 4 * KB)
    gt = sb("gt", 2 * TOK, F32, rX + 6 * KB)
    G_hi = sb("G_hi", 2 * TOK, F32R, rX + 8 * KB)
    G_lo = sb("G_lo", 2 * TOK, F32R, rX + 10 * KB)
    qrow = sb("qrow", NS * D, F32, rA)
    krow = sb("krow", NS * D, F32, rA + 8 * KB)
    vrow = sb("vrow", NS * D, F32, rA + 16 * KB)
    rope_t = sb("rope_t", D, F32, rA + 24 * KB)
    rope_u = sb("rope_u", D, F32, rA + 28 * KB)
    qT = sb("qT", KD * TOK, F32, rB)
    kT = sb("kT", KD * 3 * T, F32, rB + 8 * KB)
    cache = sb("cache", 2 * D, F32, rB + 20 * KB)
    Ea = [sb("Ea0", 4 * T, F32, rA + 24 * KB), sb("Ea1", 4 * TOK, F32, rB + 28 * KB)]
    Sa = sb("Sa", 4 * TOK, F32, rX)
    PTa = sb("PTa", 4 * TOK, F32, rX + 4 * KB)
    bias = sb("bias", NH * T, F32, rX + 8 * KB)
    fw = sb("fw", D, F32, rB)
    at = 192 * KB

    def small_sb(name, cols, dt=F32, rows=P):
        nonlocal at
        t = sb(name, cols, dt, at, rows)
        at += (cols * 4 + 63) // 64 * 64
        return t

    small = small_sb("small", NSMALL)
    ada_b = small_sb("ada_b", 512)
    mod_b = small_sb("mod_b", 512)
    modT = small_sb("modT", 64)
    diag = small_sb("diag", NS * T)
    coef_a = small_sb("coef_a", KD * NS)
    coef_b = small_sb("coef_b", KD * NS)
    cond = small_sb("cond", KD * NS)
    cond_wide = small_sb("cond_wide", KD * ADA_W, F32R)
    ssq = small_sb("ssq", NS)
    var = small_sb("var", NS)
    rstd = small_sb("rstd", NS)
    half_pow = small_sb("half_pow", NS)
    bn = small_sb("bn", NS * 6)
    mv = small_sb("mv", NS * 2)
    ccol = small_sb("ccol", NS * 36)
    gI, gF, gA, gM, gb, gc, gG = (small_sb(n, TOK) for n in ("gI", "gF", "gA", "gM", "gb", "gc", "gG"))
    g16 = small_sb("g16", TOK)
    gz = small_sb("gz", T)
    RB = small_sb("RB", 2 * TOK)
    RBW = small_sb("RBW", T)
    n_out = small_sb("n_out", 2 * DK)
    m_out = small_sb("m_out", 1)
    nsink = small_sb("nsink", NH)
    mx = small_sb("mx", 4)
    nm = small_sb("nm", 4)
    sums = small_sb("sums", 4)
    esink = small_sb("esink", 4)
    rsum = small_sb("rsum", 4)
    credit = small_sb("credit", 8)
    assert base + at <= nc.sbuf_usable_end, (base, at)

    ps = [nc.alloc_psum_tensor(f"ps{b}", [P, 512], F32) for b in range(8)]
    ACC, UP, ADA_PS, MISC = ps[0:4], ps[4:6], ps[6], ps[7]
    SCORES = [(UP[1], MISC), (ACC[0], ACC[1])]

    def sc(name, k=0, n=1, rows=P, r0=0):
        return small[r0:r0 + rows, COL[name] + k:COL[name] + k + n]

    ident = small[:, COL["ident"]:COL["ident"] + P]

    def v3(ap, b):
        return ap.rearrange("p (a b) -> p a b", b=b)

    names = """raw0 raw1 raw2 raw3 hi_done lo_done half_used
        loads x_loaded cond_silu cond_zero cond_hi cond_lo misc_init
        adab_landed modb_done modT_mm modT_done gate_mm gate_evac
        ssq_done pool_chain rstd_done diag_done nt_done hm_done hf_done hhi_done h_done x_done dve_link
        xm_hi t1_done conv_half conv_done xc_done xc_hi xc_lo xcs_done
        wg_landed wg_hi_done wg_done gates_mm g16_done rows_landed row_dve row_act c_mm
        qk_evac st_mm st_evac v_evac_a v_evac_d
        bc_mm arg_done e_done em_done qs_done p_done den_mm qs2_done qs_hi_done pt_done var_done
        rstd2_done hn_done ht_mm hc_done kw_done cn_mm cn_evac n_mm n_evac c_landed n_landed m_done m_landed
        z_silu z_mul z_hi z_lo
        tg_done cg_half cg_done tv_done cv_half cv_done sg_done gt_done ghi_done glo_done
        cache_landed bias_landed row_q_a row_q_d row_k row_v roped tq_mm tq_evac tk_mm tk_evac kv_landed
        s_mm nm_done exp_done esink_in esink_done rsum_done pn_done pt_mm pt_evac o_mm o_hi o_lo
        fw_landed final_done y_landed""".split()
    S = {n: nc.alloc_semaphore(n) for n in names}
    raw_landed = [S[f"raw{r}"] for r in range(RAW)]

    def split_hi(act, n, adv=0):
        if n >= NT:
            return
        act.wait_ge(raw_landed[n % RAW], 16 * (n // RAW + 1) + adv * 4)
        for h in range(2):
            m = 2 * n + h
            if m >= SPL:
                act.wait_ge(S["half_used"], m - SPL + 1 + adv * 2)
            act.activation(spl_hi[m % SPL][:, :], raw[n % RAW][:, h * HALF:(h + 1) * HALF],
                           ACT.Copy).then_inc(S["hi_done"], 1)

    def split_lo(dve, n, adv=0):
        if n >= NT:
            return
        for h in range(2):
            m = 2 * n + h
            dve.wait_ge(S["hi_done"], m + 1 + adv * 2)
            dve.tensor_tensor(spl_lo[m % SPL][:, :], raw[n % RAW][:, h * HALF:(h + 1) * HALF],
                              spl_hi[m % SPL][:, :].bitcast(F32), ALU.subtract).then_inc(S["lo_done"], 1)

    def tile_used(eng, n, adv=0):
        eng.wait_ge(S["half_used"], 2 * n + 2 + adv * 2)

    def out_half(t, g, s, e):
        return t[HD * e:HD * e + HD, 2 * g * TOK:(2 * g + 2) * TOK].rearrange("p (a s t) -> p a s t", s=2,
                                                                              t=T)[:, :, s, :]

    def psum_half(e):
        return UP[0][HD * e:HD * e + HD, :].rearrange("p (a e t) -> p a e t", e=2, t=T)[:, :, e, :]

    class Link:
        def __init__(self, eng, name):
            self.eng, self.sem, self.n = eng, S[name], 0

        def __call__(self, ins):
            ins.then_inc(self.sem, 1)
            self.n += 1

        def wait(self):
            self.eng.wait_ge(self.sem, self.n)

    with nc.Block() as block:

        @block.sync
        def _(sp):
            for n in range(RAW):
                sp.dma_start(raw[n][:, :], io["stream"][n]).then_inc(raw_landed[n], 16)

            def refill(n, adv=0):
                sp.wait_ge(S["lo_done"], 2 * (n - RAW) + 2 + adv * 2)
                src = io["stream"][n] if isinstance(adv, int) else \
                    io["stream"][bass.ds(adv + n, 1)].rearrange("a p n -> p (a n)")
                sp.dma_start(raw[n % RAW][:, :], src).then_inc(raw_landed[n % RAW], 16)

            rounds = NT // RAW - 1
            with sp.Fori(0, rounds) as it:
                for r in range(RAW):
                    refill(RAW + r, it * RAW)
            for n in range((rounds + 1) * RAW, NT):
                refill(n)

        @block.tensor
        def _(pe):
            def weights_stationary(n, adv, chunk, k0, bank, first, last, norm=None):
                for h in range(2):
                    m = 2 * n + h
                    pe.wait_ge(S["lo_done"], m + 1 + adv * 2)
                    if norm is not None:
                        pe.wait_ge(S["h_done"], 4 * norm + 2 * h + 2)
                    for b in range(2):
                        for k in range(4):
                            c = slice(k * 256 + b * P, k * 256 + b * P + P)
                            w_hi, w_lo = spl_hi[m % SPL][:, c], spl_lo[m % SPL][:, c]
                            x_hi, x_lo = chunk(k0 + 4 * h + k)
                            out = bank[:, b * TOK:(b + 1) * TOK]
                            st = first and h == 0 and b == 0 and k == 0
                            en = last and h == 1 and b == 1 and k == 3
                            pe.matmul(out, w_hi, x_hi, start=st, stop=False, skip_group_check=True)
                            pe.matmul(out, w_hi, x_lo, start=False, stop=False, skip_group_check=True)
                            mm = pe.matmul(out, w_lo, x_hi, start=False, stop=en, skip_group_check=True)
                    mm.then_inc(S["half_used"], 1)

            def rows_stationary(n, adv, chunk, first, last, width=1024, banks=None):
                for h in range(2):
                    m = 2 * n + h
                    pe.wait_ge(S["lo_done"], m + 1 + adv * 2)
                    per = HALF // width
                    for k in range(per):
                        for s in range(NS):
                            a_hi, a_lo = chunk(per * h + k, s)
                            for a, parts in ((a_hi, (spl_hi, spl_lo)), (a_lo, (spl_hi,))):
                                for w in parts:
                                    for c in range(width // 512):
                                        out = (banks or ACC)[s * (width // 512) + c]
                                        st = first and h == 0 and k == 0 and a is a_hi and w is spl_hi
                                        en = last and h == 1 and k == per - 1 and a is a_lo
                                        o = k * width + c * 512
                                        mm = pe.matmul(out[:, :], a, w[m % SPL][:, o:o + 512], start=st, stop=en,
                                                       skip_group_check=True)
                    mm.then_inc(S["half_used"], 1)

            def ada_start(i, phase):
                if 3 * i + phase:
                    pe.wait_ge(S["modb_done"], 3 * i + phase)
                pe.matmul(ADA_PS[0:ADA_M, 0:8], cond_wide[:, 16:16 + ADA_M], cond_wide[:, 16:24], start=True,
                          stop=False, skip_group_check=True)

            def ada(n, i, g, adv=0, col=0):
                phase = g // ADA_PHASE
                out = ADA_PS[0:ADA_M, bass.ds(col + 256 * (g // 4 % 2), 256)]
                o = 12 - 4 * (g % 4)
                if phase and g % ADA_PHASE == 0:
                    ada_start(i, phase)
                for h in range(2):
                    m = 2 * n + h
                    pe.wait_ge(S["lo_done"], m + 1 + adv * 2)
                    for k in range(4):
                        c = cond_wide[:, ADA_W * (4 * h + k) + o:ADA_W * (4 * h + k) + o + ADA_M]
                        for w in (spl_hi, spl_lo):
                            mm = pe.matmul(out, c, w[m % SPL][:, k * 256:(k + 1) * 256], start=False,
                                           stop=h == 1 and k == 3 and w is spl_lo, skip_group_check=True)
                    mm.then_inc(S["half_used"], 1)

            def col(t, k, s=None):
                o = k * TOK + (0 if s is None else s * T)
                return t[:, o:o + (TOK if s is None else T)]

            def both(hi, lo):
                return lambda k, s=None: (col(hi, k, s), col(lo, k, s))

            def norm(q):
                rows = 16 if q % 2 == 0 else MOD_ROWS
                pe.wait_ge(S["modb_done"], 3 * (q // 2) + (3 if q % 2 else 1))
                if q:
                    pe.wait_ge(S["gate_evac"], 4 * q)
                for b in range(4):
                    mm = pe.transpose(MISC[:, b * MOD_ROWS:b * MOD_ROWS + rows], mod_b[0:rows, b * P:(b + 1) * P],
                                      ident[0:rows, 0:rows])
                mm.then_inc(S["modT_mm"], 1)
                pe.wait_ge(S["diag_done"], 2 * q + 2)
                for g in range(4):
                    for k in range(2):
                        for s in range(NS):
                            o = (k * 2 + s) * T
                            mm = pe.matmul(ACC[g][:, o:o + T],
                                           x[:, s * D + (2 * g + k) * P:s * D + (2 * g + k + 1) * P],
                                           diag[:, s * T:(s + 1) * T], start=k == 0 and s == 0, stop=k == 1 and s == 1,
                                           skip_group_check=True)
                    mm.then_inc(S["nt_done"], 1)

            def gate(r, b):
                s, c = b // 2, b % 2
                row, column = GATE2 if r % 2 else GATE1
                if b == 0:
                    pe.wait_ge(S["modT_done"], r + 1)
                    if r % 2 == 0:
                        pe.wait_ge(S["modb_done"], 3 * (r // 2) + 2)
                    if MIXER[r // 2] == "mlstm":
                        pe.wait_ge(S["n_evac"], MH * (ML_INDEX[r // 2] + 1))
                if 4 * r + b:
                    pe.wait_ge(S["gate_evac"], 4 * r + b)
                for k in range(2):
                    sel = small[row:row + 16, COL["gate_sel"] + 2 * (2 * c + k) + s:COL["gate_sel"] + 2 * (2 * c + k) + s + 1]
                    mm = pe.matmul(MISC[:, k * 256:(k + 1) * 256], sel.to_broadcast([16, P]),
                                   mod_b[row:row + 16, column:column + 256], start=k == 0, stop=k == 1,
                                   skip_group_check=True)
                mm.then_inc(S["gate_mm"], 1)

            def mlstm(i):
                j = ML_INDEX[i]
                n0 = INDEX["ml_x", i, 0]
                with pe.Fori(0, 2) as it:
                    for t in range(4):
                        pe.wait_ge(S["conv_done"], 8 * j + t + 1 + it * 4)
                        weights_stationary(n0 + t, it * 4, both(H_hi, H_lo), 0, UP[t % 2], True, True,
                                           2 * i if t == 0 else None)
                pe.wait_ge(S["wg_done"], j + 1)
                pe.wait_ge(S["xc_lo"], 2 + 8 * (j + 1))
                for k in range(KI):
                    w_hi, w_lo = wg_hi[:, 16 * k:16 * k + 16], wg_lo[:, 16 * k:16 * k + 16]
                    a_hi, a_lo = both(A_hi, A_lo)(k)
                    pe.matmul(MISC[0:16, 0:TOK], w_hi, a_hi, start=k == 0, stop=False)
                    pe.matmul(MISC[0:16, 0:TOK], w_hi, a_lo, start=False, stop=False)
                    mm = pe.matmul(MISC[0:16, 0:TOK], w_lo, a_hi, start=False, stop=k == KI - 1)
                mm.then_inc(S["gates_mm"], 1)
                n0 = INDEX["ml_qk", i, 0, 0]
                for part in range(2):
                    with pe.Fori(0, 2) as it:
                        for t in range(4):
                            if t % 2 == 0:
                                pe.wait_ge(S["qk_evac"], 8 * j + 4 * part + t // 2 + 1 + it * 2)
                            weights_stationary(n0 + 8 * part + t, it * 4, both(B_hi, B_lo), 8 * (t % 2),
                                               UP[(t // 2) % 2], t % 2 == 0, t % 2 == 1)
                pe.wait_ge(S["qk_evac"], 2 + 8 * (j + 1))
                for b in range(2):
                    for hs in range(4 * b, 4 * b + 4):
                        h, s = hs // 2, hs % 2
                        for c in range(2):
                            mm = pe.matmul(ACC[b][:, (hs % 4) * T:(hs % 4 + 1) * T], col(K, 2 * h + c, s),
                                           col(Q, 2 * h + c, s), start=hs % 4 == 0 and c == 0, stop=c == 1,
                                           skip_group_check=True)
                    mm.then_inc(S["st_mm"], 1)
                for b in range(2):
                    for c in range(4):
                        mm = pe.transpose(ACC[2 + b][:, c * P:(c + 1) * P], col(K, 4 * b + c, 0), ident)
                    mm.then_inc(S["st_mm"], 1)
                pe.wait_ge(S["row_dve"], ROW_DVE * j + ROW_C)
                for s in range(NS):
                    mm = pe.transpose(MISC[:, 36 * s:36 * s + 36], gc[0:36, s * T:(s + 1) * T], ident[0:36, 0:36])
                mm.then_inc(S["c_mm"], 1)
                n0 = INDEX["ml_v", i, 0, 0]
                for half in range(2):
                    if half == 0:
                        pe.wait_ge(S["st_evac"], 4 * (j + 1))
                    else:
                        pe.wait_ge(S["v_evac_a"], 4 * j + 2)
                        pe.wait_ge(S["v_evac_d"], 4 * j + 2)
                    for t in range(8):
                        rows_stationary(n0 + 8 * half + t, 0, lambda k, s: both(A_hi, A_lo)(2 * t + k, s),
                                        t == 0, t == 7)
                for h in range(MH):
                    head(i, j, h)
                n0 = INDEX["ml_z", i, 0]
                pe.wait_ge(S["hc_done"], 4 * (j + 1))
                with pe.Fori(0, 2) as it:
                    for t in range(4):
                        pe.wait_ge(S["z_silu"], 8 * j + t + 1 + it * 4)
                        weights_stationary(n0 + t, it * 4, both(H_hi, H_lo), 0, UP[t % 2], True, True)
                pe.wait_ge(S["z_lo"], 2 + 8 * (j + 1))
                n0 = INDEX["ml_down", i, 0]
                for t in range(8):
                    rows_stationary(n0 + t, 0, lambda k, s: both(A_hi, A_lo)(2 * t + k, s), t == 0, t == 7)
                    if t < 4:
                        gate(2 * i, t)

            def gate_rows(h):
                for d in range(2):
                    pe.matmul(UP[d][:, :], ident[0:36, 32 * d + h:32 * d + h + 1].to_broadcast([36, P]), RB[0:36, :],
                              start=True, stop=True)

            def head(i, j, h):
                q = 4 * j + h
                n = INDEX["ml_C", i, h]
                if q:
                    pe.wait_ge(S["n_evac"], q)
                if h == 0:
                    pe.wait_ge(S["v_evac_a"], 4 * (j + 1))
                    pe.wait_ge(S["v_evac_d"], 4 * (j + 1))
                    pe.wait_ge(S["row_dve"], ROW_DVE * (j + 1))
                    pe.wait_ge(S["row_act"], ROW_ACT * (j + 1))
                    gate_rows(0)
                for d in range(2):
                    mm = pe.matmul(ACC[0][:, d * T:(d + 1) * T],
                                   ident[0:36, 32 * d + h:32 * d + h + 1].to_broadcast([36, P]), RBW[0:36, :],
                                   start=d == 0, stop=d == 1, skip_group_check=True)
                mm.then_inc(S["bc_mm"], 1)
                for m in (n - 2, n - 1):
                    ada(m, i, ORDER[m][2])
                pe.wait_ge(S["p_done"], q + 1)
                pe.wait_ge(S["qs_done"], q + 1)
                pe.matmul(ACC[1][:, :], sc("ones").to_broadcast([P, P]), Pw[:, :], start=True, stop=False,
                          skip_group_check=True)
                for d in range(2):
                    for c in range(2):
                        o = 16 * j + (4 * d + h) * 2 + c
                        mm = pe.matmul(ACC[1][:, (2 * d + 1) * T:(2 * d + 2) * T],
                                       sc("n0", o).to_broadcast([P, P]), qs[:, (2 * d + c) * T:(2 * d + c + 1) * T],
                                       start=False, stop=d == 1 and c == 1, skip_group_check=True)
                mm.then_inc(S["den_mm"], 1)
                pe.wait_ge(S["kw_done"], 2 * q + 2)
                if q:
                    pe.wait_ge(S["hc_done"], q)
                for d in range(2):
                    for c in range(2):
                        e = 4 * q + 2 * d + c
                        if e >= 2:
                            pe.wait_ge(S["cn_evac"], e - 1)
                        pe.matmul(ACC[2 + c][:, :], kw[:, d * DK + c * P:d * DK + (c + 1) * P],
                                  v[:, h * DV:(h + 1) * DV], start=True, stop=True).then_inc(S["cn_mm"], 1)
                for d in range(2):
                    last = d * TOK + (T - 1 if d == 0 else 0)
                    mm = pe.matmul(MISC[0:1, d * DK:(d + 1) * DK], E[:, last:last + 1],
                                   knat[:, h * DK:(h + 1) * DK], start=d == 0, stop=d == 1, skip_group_check=True)
                mm.then_inc(S["n_mm"], 1)
                pe.wait_ge(S["pt_done"], q + 1)
                pe.matmul(ACC[0][:, :], PT[:, 0:T], v[:, h * DV:(h + 1) * DV], start=True, stop=True)
                pe.wait_ge(S["qs_hi_done"], q + 1)
                pe.wait_ge(S["qs2_done"], 2 * q + 2)
                pe.matmul(ACC[1][:, :], PT[:, T:TOK], v[:, DIN + h * DV:DIN + (h + 1) * DV], start=True, stop=False,
                          skip_group_check=True)
                for d in range(2):
                    m = 2 * n + d
                    pe.wait_ge(S["lo_done"], m + 1)
                    for c in range(2):
                        o = slice((2 * d + c) * T, (2 * d + c + 1) * T)
                        for a, w in ((qs_hi, spl_hi), (qs_hi, spl_lo), (qs_lo, spl_hi)):
                            mm = pe.matmul(ACC[1][:, :], a[:, o], w[m % SPL][:, c * DV:(c + 1) * DV], start=False,
                                           stop=d == 1 and c == 1 and a is qs_lo, skip_group_check=True)
                    mm.then_inc(S["half_used"], 1)
                for m in (n + 1, n + 2):
                    ada(m, i, ORDER[m][2])
                if h + 1 < MH:
                    pe.wait_ge(S["em_done"], 2 * q + 2)
                    gate_rows(h + 1)
                pe.wait_ge(S["hn_done"], 2 * q + 2)
                pe.wait_ge(S["cn_evac"], 4 * q + 4)
                for f in range(4):
                    for s in range(NS):
                        o = ((f % 2) * 2 + s) * T
                        mm = pe.transpose(ACC[2 + f // 2][:, o:o + T], hn[:, s * DV + f * P:s * DV + (f + 1) * P], ident)
                mm.then_inc(S["ht_mm"], 1)

            def attention(i):
                a = i - 1
                nb = 4 if a == 0 else 8
                pe.wait_ge(S["hf_done"], 8 * i + 4)
                if a == 0:
                    n0 = INDEX["q", i, 0]
                    for t in range(4):
                        pe.wait_ge(S["h_done"], 8 * i + t + 1)
                        rows_stationary(n0 + t, 0, lambda k, s: both(H_hi, H_lo)(2 * t + k, s), t == 0, t == 3)
                    n0 = INDEX["kv", i, 0]
                    for t in range(2):
                        rows_stationary(n0 + t, 0, lambda k, s: both(H_hi, H_lo)(4 * t + k, s), t == 0, t == 1,
                                        width=512, banks=UP)
                else:
                    for c in range(3):
                        if c:
                            pe.wait_ge(S["row_q_a"], 2 + 2 * c)
                            pe.wait_ge(S["row_q_d"], 2 + 2 * c)
                        n0 = INDEX["qkv", i, c, 0]
                        for t in range(4):
                            pe.wait_ge(S["h_done"], 8 * i + t + 1)
                            rows_stationary(n0 + t, 0, lambda k, s: both(H_hi, H_lo)(2 * t + k, s), t == 0, t == 3)
                pe.wait_ge(S["row_q_a"], 2 if a == 0 else 8)
                pe.wait_ge(S["row_q_d"], 2 if a == 0 else 8)
                pe.wait_ge(S["roped"], 1)
                for b in range(4):
                    for p in range(4):
                        pr, s = 2 * b + p // 2, p % 2
                        mm = pe.transpose(ACC[b][:, p * T:(p + 1) * T], qrow[:, s * D + pr * P:s * D + (pr + 1) * P],
                                          ident)
                    mm.then_inc(S["tq_mm"], 1)
                pe.wait_ge(S["roped"], 2)
                pe.wait_ge(S["cache_landed"], 16 * (a + 1))
                for b in range(3 * nb // 4):
                    bank = UP[b % 2]
                    if b >= 2:
                        pe.wait_ge(S["tk_evac"], 3 * a + b - 1)
                    elif a == 0:
                        pe.wait_ge(S["row_k"], 2)
                        pe.wait_ge(S["row_v"], 2)
                    for p in range(4):
                        blk, src = divmod(4 * b + p, 3)
                        rows = cache[:, blk * P:(blk + 1) * P] if src == 2 else \
                            krow[:, src * nb * P + blk * P:src * nb * P + (blk + 1) * P]
                        mm = pe.transpose(bank[:, p * T:(p + 1) * T], rows, ident)
                    mm.then_inc(S["tk_mm"], 1)
                pe.wait_ge(S["tq_evac"], 4 * (a + 1))
                pe.wait_ge(S["tk_evac"], 3 * a + 3 * nb // 4)
                n = INDEX["ada", i, ADA_PHASE]

                def scores(u):
                    g, s = u // 2, u % 2
                    w = 8 * a + u
                    if w >= 2:
                        pe.wait_ge(S["exp_done"], 4 * w - 4)
                        pe.wait_ge(S["nm_done"], w - 1)
                    width = (1 + s) * T
                    for p in range(4):
                        hd = HEAD_ORDER[4 * g + p]
                        r0 = HD * (hd % 2)
                        blk = hd // 4 if a == 0 else hd // 2
                        q_ = qT[r0:r0 + HD, (hd // 2) * TOK + s * T:(hd // 2) * TOK + (s + 1) * T]
                        mm = pe.matmul(SCORES[s][p // 2][:, (p % 2) * width:(p % 2 + 1) * width], q_,
                                       kT[r0:r0 + HD, blk * 3 * T + s * T:blk * 3 * T + s * T + width],
                                       start=p % 2 == 0, stop=p % 2 == 1, skip_group_check=True)
                    mm.then_inc(S["s_mm"], 1)

                scores(0)
                for u in range(8):
                    g, s = u // 2, u % 2
                    w = 8 * a + u
                    if u < 7:
                        scores(u + 1)
                    for m in (n + 2 * u, n + 2 * u + 1):
                        ada(m, i, ORDER[m][2])
                    pe.wait_ge(S["pn_done"], w + 1)
                    for b in range(1 + s):
                        for p in range(4):
                            o = (4 * b + p) * T
                            mm = pe.transpose(ACC[2 + b][:, p * T:(p + 1) * T], Ea[s][:, o:o + T], ident)
                        mm.then_inc(S["pt_mm"], 1)
                    pe.wait_ge(S["pt_evac"], 3 * (w // 2) + 1 + 2 * s)
                    if w:
                        pe.wait_ge(S["o_lo"], 2 * w)
                    for p in range(4):
                        hd = HEAD_ORDER[4 * g + p]
                        k = hd % 4
                        blk = hd // 4 if a == 0 else hd // 2
                        for e in range(1 + s):
                            o = (p * (1 + s) + e) * T
                            vals = cache[:, (nb + blk) * P:(nb + blk + 1) * P] if e else \
                                vrow[:, s * nb * P + blk * P:s * nb * P + (blk + 1) * P]
                            mm = pe.matmul(UP[0][:, k * T:(k + 1) * T], vals, PTa[:, o:o + T],
                                           start=p == 0 and e == 0, stop=e == s, skip_group_check=True)
                    mm.then_inc(S["o_mm"], 1)
                pe.wait_ge(S["o_lo"], 16 * (a + 1))
                n0 = INDEX["o", i, 0]
                for t in range(4):
                    rows_stationary(n0 + t, 0, lambda k, s: both(H_hi, H_lo)(2 * t + k, s), t == 0, t == 3)
                    if t < 3:
                        gate(2 * i, t)
                    if t == 2:
                        gate(2 * i, 3)

            def ffn(i):
                n0 = INDEX["ffn_up", i, 0]
                mine = lambda k, s: (col(G_hi, k, s), col(G_lo, k, s))

                def step(j, n, adv=0, jj=0, g=None, col=0):
                    if NJ * i + j > 0:
                        pe.wait_ge(S["cg_done"], NJ * i + j + jj)
                    weights_stationary(n, adv, both(H_hi, H_lo), 0, UP[0], True, True, 2 * i + 1 if j == 0 else None)
                    if j < 2:
                        gate(2 * i + 1, 2 * j)
                    if NJ * i + j > 0:
                        pe.wait_ge(S["cv_done"], NJ * i + j + jj)
                    weights_stationary(n + 1, adv, both(H_hi, H_lo), 0, UP[1], True, True)
                    if j < 2:
                        gate(2 * i + 1, 2 * j + 1)
                    if j > 0:
                        pe.wait_ge(S["glo_done"], NJ * i + j + jj)
                        rows_stationary(n + 2, adv, mine, j == 1, False)
                    if g is not None:
                        ada(n + 3, i + 1, g, adv, col)

                per = 4 if i + 1 < DEPTH else 3
                if i + 1 < DEPTH:
                    ada_start(i + 1, 0)
                step(0, n0)
                step(1, n0 + 2)
                with pe.Fori(0, 2) as it:
                    for r in range(4):
                        step(2 + r, n0 + 5 + per * r, it * (4 * per), it * 4, r if per == 4 else None, it * 256)
                step(10, n0 + 5 + 8 * per)
                pe.wait_ge(S["glo_done"], NJ * (i + 1))
                rows_stationary(INDEX["ffn_down", i, NJ - 1], 0, mine, False, True)

            pe.wait_ge(S["misc_init"], 1)
            pe.wait_ge(S["cond_lo"], 1)
            ada_start(0, 0)
            for g in range(ADA_PHASE):
                ada(g, 0, g)
            for i in range(DEPTH):
                norm(2 * i)
                if MIXER[i] == "mlstm":
                    mlstm(i)
                else:
                    attention(i)
                norm(2 * i + 1)
                ffn(i)

        @block.scalar
        def _(act):
            def copy(out, in_, sem, scale=1.0):
                act.activation(out, in_, ACT.Copy, scale=scale).then_inc(S[sem], 1)

            def squares(q):
                for s in range(NS):
                    if q == 0:
                        act.wait_ge(S["x_loaded"], 16)
                    else:
                        act.wait_ge(S["x_done"], 2 * q - 1 + s)
                    act.activation(xn[:, s * D:(s + 1) * D], x[:, s * D:(s + 1) * D], ACT.Square,
                                   accum_out=ssq[:, s:s + 1]).then_inc(S["ssq_done"], 1)

            def norm(q):
                squares(q)
                for g in range(4):
                    act.wait_ge(S["hf_done"], 4 * q + g + 1)
                    copy(H_hi[:, g * 512:(g + 1) * 512], hf[g % 2][:, :], "hhi_done")

            def gate(r, b):
                act.wait_ge(S["h_done"], 4 * r + 4)
                act.wait_ge(S["gate_mm"], 4 * r + b + 1)
                copy(gate_bc[:, b * 512:(b + 1) * 512], MISC[:, :], "gate_evac")

            def splits(n0, count):
                if count >= 8:
                    with act.Fori(0, count // 4) as it:
                        for t in range(4):
                            split_hi(act, n0 + t + 1, it * 4)
                else:
                    for t in range(count):
                        split_hi(act, n0 + t + 1)

            def part(t, base_, it):
                return t[:, bass.ds(it * 4 * 512 + base_ * 512, 512)]

            def mlstm(i):
                j = ML_INDEX[i]
                act.dma_start(wg_raw[:, :], io["w_gate"][j]).then_inc(S["wg_landed"], 16)
                n0 = INDEX["ml_x", i, 0]

                def silu_hi(t, it):
                    act.wait_ge(S["conv_done"], 2 + 8 * j + t + 1 + it * 4)
                    act.wait_ge(S["xc_lo"], 8 * j + t + 1 + it * 4)
                    act.wait_ge(S["xcs_done"], 8 * j + t + 1 + it * 4)
                    act.activation(ow[t % 2][:, :], t1[t % 2][:, :], ACT.Silu).then_inc(S["xc_done"], 1)
                    act.wait_ge(S["xc_done"], 8 * j + t + 1 + it * 4)
                    copy(part(B_hi, t, it), ow[t % 2][:, :], "xc_hi")

                with act.Fori(0, 2) as it:
                    for t in range(4):
                        split_hi(act, n0 + t + 1, it * 4)
                        tile_used(act, n0 + t, it * 4)
                        copy(part(A_hi, t, it), UP[t % 2][:, :], "xm_hi")
                        for b in range(2):
                            w = COL["ml_conv_w"] + (3 * j + 1) * KI + 2 * t + b
                            c = COL["ml_conv_b"] + j * KI + 2 * t + b
                            act.activation(t1[t % 2][:, b * TOK:(b + 1) * TOK], UP[t % 2][:, b * TOK:(b + 1) * TOK],
                                           ACT.Identity, bias=small[:, bass.ds(it * 8 + c, 1)],
                                           scale=small[:, bass.ds(it * 8 + w, 1)]).then_inc(S["t1_done"], 1)
                        if t:
                            silu_hi(t - 1, it)
                    silu_hi(3, it)
                act.wait_ge(S["wg_landed"], 16 * (j + 1))
                copy(wg_hi[:, :], wg_raw[:, :], "wg_hi_done")
                n0 = INDEX["ml_qk", i, 0, 0]
                for g in range(4):
                    split_hi(act, n0 + 2 * g + 1)
                    if g == 0:
                        act.wait_ge(S["gates_mm"], j + 1)
                        act.activation(g16[0:16, :], MISC[0:16, 0:TOK], ACT.Identity,
                                       bias=sc("b_gate", j, rows=16)).then_inc(S["g16_done"], 1)
                        act.wait_ge(S["g16_done"], j + 1)
                        if j:
                            act.wait_ge(S["row_dve"], ROW_DVE * j)
                        for k, (t, r) in enumerate([(gI, 0), (gF, 0), (gI, 32), (gF, 32)]):
                            act.dma_start(t[r:r + 4, :], g16[4 * k:4 * k + 4, :]).then_inc(S["rows_landed"], 16)
                    if g == 1:
                        act.wait_ge(S["row_dve"], ROW_DVE * j + ROW_ABS)
                        act.activation(gA[0:36, :], gA[0:36, :], ACT.Exp, scale=-1.0).then_inc(S["row_act"], 1)
                        act.wait_ge(S["row_act"], ROW_ACT * j + 1)
                        act.activation(gA[0:36, :], gA[0:36, :], ACT.Ln, bias=1.0).then_inc(S["row_act"], 1)
                    if g == 3:
                        act.wait_ge(S["row_dve"], ROW_DVE * j + ROW_G)
                        act.activation(RBW[0:36, :], RB[0:36, T:TOK], ACT.Exp,
                                       bias=sc("m0", j, rows=36)).then_inc(S["row_act"], 1)
                    split_hi(act, n0 + 2 * g + 2)
                    tile_used(act, n0 + 2 * g + 1)
                    copy(Q[:, g * 512:(g + 1) * 512], UP[g % 2][:, :], "qk_evac", scale=DK ** -0.5)
                n0 += 8
                with act.Fori(0, 2) as it:
                    for g in range(2):
                        split_hi(act, n0 + 2 * g + 1, it * 4)
                        split_hi(act, n0 + 2 * g + 2, it * 4)
                        tile_used(act, n0 + 2 * g + 1, it * 4)
                        copy(K[:, bass.ds(it * 1024 + g * 512, 512)], UP[g % 2][:, :], "qk_evac")
                act.wait_ge(S["m_done"], 2 * (j + 1))
                for d in range(2):
                    act.dma_start(io["new_m"][0, j, d:d + 1, :].rearrange("a h -> h a"),
                                  m_out[32 * d:32 * d + MH, :]).then_inc(S["m_landed"], 16)
                for half in range(2):
                    n0 = INDEX["ml_v", i, half, 0]
                    splits(n0, 8)
                    tile_used(act, n0 + 7)
                    for c in range(2):
                        copy(v[:, half * 1024 + c * 512:half * 1024 + (c + 1) * 512], ACC[c][:, :], "v_evac_a")
                for h in range(MH):
                    head(i, j, h)
                n0 = INDEX["ml_z", i, 0]

                def z_hi(t, it):
                    act.wait_ge(S["z_mul"], 2 + 8 * j + t + 1 + it * 4)
                    copy(part(A_hi, t, it), ow[t % 2][:, :], "z_hi")

                with act.Fori(0, 2) as it:
                    for t in range(4):
                        split_hi(act, n0 + t + 1, it * 4)
                        tile_used(act, n0 + t, it * 4)
                        act.wait_ge(S["z_mul"], 8 * j + t + 1 + it * 4)
                        act.activation(t1[t % 2][:, :], UP[t % 2][:, :], ACT.Silu).then_inc(S["z_silu"], 1)
                        if t:
                            z_hi(t - 1, it)
                    z_hi(3, it)
                n0 = INDEX["ml_down", i, 0]
                for t in range(8):
                    split_hi(act, n0 + t + 1)
                    if t < 4:
                        gate(2 * i, t)

            def head(i, j, h):
                q = 4 * j + h
                n = INDEX["ml_C", i, h]
                split_hi(act, n - 1)
                act.wait_ge(S["arg_done"], 2 * q + 2)
                for d in range(2):
                    for s in range(NS):
                        o = (2 * d + s) * T
                        act.activation(E[:, o:o + T], E[:, o:o + T], ACT.Exp,
                                       bias=ccol[:, 36 * s + 32 * d + h:36 * s + 32 * d + h + 1]
                                       ).then_inc(S["e_done"], 1)
                if q:
                    act.wait_ge(S["pt_done"], q)
                for d in range(2):
                    act.activation(Em[:, d * TOK:(d + 1) * TOK], UP[d][:, TOK:2 * TOK],
                                   ACT.Exp).then_inc(S["em_done"], 1)
                act.wait_ge(S["e_done"], 4 * q + 4)
                for d in range(2):
                    last = d * TOK + (T - 1 if d == 0 else 0)
                    act.activation(kw[:, d * DK:(d + 1) * DK], knat[:, h * DK:(h + 1) * DK], ACT.Identity,
                                   scale=E[:, last:last + 1]).then_inc(S["kw_done"], 1)
                split_hi(act, n)
                split_hi(act, n + 1)
                if q:
                    act.wait_ge(S["c_landed"], 32 * q)
                for e in range(4):
                    act.wait_ge(S["cn_mm"], 4 * q + e + 1)
                    copy(c_stage[:, e * DV:(e + 1) * DV], ACC[2 + e % 2][:, :], "cn_evac")
                act.wait_ge(S["cn_evac"], 4 * q + 4)
                for d in range(2):
                    act.dma_start(io["new_C"][0, j, d, h].rearrange("(c p) v -> p c v", p=P),
                                  v3(c_stage[:, d * HALF:(d + 1) * HALF], DV)).then_inc(S["c_landed"], 16)
                act.wait_ge(S["n_mm"], q + 1)
                if q:
                    act.wait_ge(S["n_landed"], 16 * q)
                copy(n_out[0:1, :], MISC[0:1, :], "n_evac")
                act.wait_ge(S["n_evac"], q + 1)
                act.dma_start(io["new_n"][0, j, :, h].rearrange("(a d) k -> a d k", a=1),
                              n_out[0:1, :].rearrange("p (d k) -> p d k", d=2)).then_inc(S["n_landed"], 16)
                act.wait_ge(S["qs2_done"], 2 * q + 1)
                copy(qs_hi[:, :], qs[:, :], "qs_hi_done")
                split_hi(act, n + 2)
                split_hi(act, n + 3)

            def attention(i):
                a = i - 1
                nb = 4 if a == 0 else 8
                name = "swa" if a == 0 else "na"
                act.dma_start(cache[:, 0:2 * nb * P], io[name + "_cache"]).then_inc(S["cache_landed"], 16)
                if a == 0:
                    n0 = INDEX["q", i, 0]
                    splits(n0, 4)
                    tile_used(act, n0 + 3)
                    for c in range(2):
                        copy(qrow[:, c * 512:(c + 1) * 512], ACC[c][:, :], "row_q_a")
                    n0 = INDEX["kv", i, 0]
                    splits(n0, 2)
                    act.wait_ge(S["row_k"], 2)
                    for s in range(NS):
                        copy(vrow[:, s * 512:(s + 1) * 512].rearrange("p (h e d) -> p h e d", e=2, d=HD),
                             UP[s][:, 256:512].rearrange("p (h e d) -> p h e d", e=1, d=HD)
                             .to_broadcast([P, KV, 2, HD]), "row_v")
                else:
                    act.dma_start(bias[:, :], io["rpb"]).then_inc(S["bias_landed"], 16)
                    for c, rows in enumerate((qrow, krow, vrow)):
                        n0 = INDEX["qkv", i, c, 0]
                        splits(n0, 4)
                        tile_used(act, n0 + 3)
                        for k in range(2):
                            copy(rows[:, k * 512:(k + 1) * 512], ACC[k][:, :], "row_q_a")
                if a == 0:
                    act.wait_ge(S["row_v"], 1)
                    views = [t[:, 0:512].rearrange("p (h e d) -> p h e d", e=2, d=HD)[:, :, 0, :]
                             for t in (krow, vrow)]
                else:
                    act.wait_ge(S["row_q_a"], 8)
                    views = [t[:, 0:D].rearrange("p (h d) -> p h d", d=HD) for t in (krow, vrow)]
                for which, view in zip("kv", views):
                    act.dma_start(io[f"{name}_{which}"][0, 0].rearrange("h t d -> t h d"), view
                                  ).then_inc(S["kv_landed"], 16)
                for b in range(3 * nb // 4):
                    act.wait_ge(S["tk_mm"], 3 * a + b + 1)
                    copy(kT[:, b * 512:(b + 1) * 512], UP[b % 2][:, :], "tk_evac")
                n = INDEX["ada", i, ADA_PHASE]

                def exps(u):
                    s = u % 2
                    w = 8 * a + u
                    width = (1 + s) * T
                    act.wait_ge(S["nm_done"], w + 1)
                    for k in range(4):
                        if a == 1 and s == 1:
                            src, scale = Sa[:, k * width:(k + 1) * width], 1.0
                        else:
                            src, scale = SCORES[s][k // 2][:, (k % 2) * width:(k % 2 + 1) * width], HD ** -0.5
                        act.activation(Ea[s][:, k * width:(k + 1) * width], src, ACT.Exp, bias=nm[:, k:k + 1],
                                       scale=scale, accum_out=sums[:, k:k + 1]).then_inc(S["exp_done"], 1)
                    if a == 0:
                        act.wait_ge(S["esink_in"], w + 1)
                        act.activation(esink[:, :], esink[:, :], ACT.Exp).then_inc(S["esink_done"], 1)

                exps(0)
                for u in range(8):
                    g, s = u // 2, u % 2
                    w = 8 * a + u
                    split_hi(act, n + 2 * u + 1)
                    if u < 7:
                        exps(u + 1)
                    split_hi(act, n + 2 * u + 2)
                    for b in range(1 + s):
                        act.wait_ge(S["pt_mm"], 3 * (w // 2) + s + b + 1)
                        copy(PTa[:, b * 512:(b + 1) * 512], ACC[2 + b][:, :], "pt_evac")
                    act.wait_ge(S["o_mm"], w + 1)
                    for e in range(2):
                        copy(out_half(H_hi, g, s, e), psum_half(e), "o_hi")
                for t in range(4):
                    split_hi(act, INDEX["o", i, t] + 1)
                    if t < 3:
                        gate(2 * i, t)
                    if t == 2:
                        gate(2 * i, 3)

            def ffn(i):
                n0 = INDEX["ffn_up", i, 0]
                w0 = COL["ffn_conv_w"] + (3 * i + 1) * FB
                b0 = COL["ffn_conv_b"] + i * FB

                def taps(dst, bank, j, blk, jj, sem):
                    for b in range(2):
                        k = blk + 2 * j + b
                        act.activation(dst[:, b * TOK:(b + 1) * TOK], bank[:, b * TOK:(b + 1) * TOK], ACT.Identity,
                                       bias=small[:, bass.ds(jj * 2 + b0 + k, 1)],
                                       scale=small[:, bass.ds(jj * 2 + w0 + k, 1)]).then_inc(S[sem], 1)

                def step(j, n, adv=0, jj=0, with_ada=False):
                    split_hi(act, n + 1, adv)
                    tile_used(act, n, adv)
                    if NJ * i + j:
                        act.wait_ge(S["gt_done"], NJ * i + j + jj)
                    taps(tg, UP[0], j, 0, jj, "tg_done")
                    if j < 2:
                        gate(2 * i + 1, 2 * j)
                    split_hi(act, n + 2, adv)
                    tile_used(act, n + 1, adv)
                    taps(tv, UP[1], j, FB // 2, jj, "tv_done")
                    if j < 2:
                        gate(2 * i + 1, 2 * j + 1)
                    act.wait_ge(S["cg_done"], NJ * i + j + 1 + jj)
                    act.activation(sg[:, :], tg[:, :], ACT.Silu).then_inc(S["sg_done"], 1)
                    if j > 0:
                        split_hi(act, n + 3, adv)
                        tile_used(act, n + 2, adv)
                    if with_ada:
                        split_hi(act, n + 4, adv)
                    act.wait_ge(S["gt_done"], NJ * i + j + 1 + jj)
                    copy(G_hi[:, :], gt[:, :], "ghi_done")

                per = 4 if i + 1 < DEPTH else 3
                step(0, n0)
                step(1, n0 + 2)
                with act.Fori(0, 2) as it:
                    for r in range(4):
                        step(2 + r, n0 + 5 + per * r, it * (4 * per), it * 4, per == 4)
                step(10, n0 + 5 + 8 * per)
                split_hi(act, INDEX["ffn_down", i, NJ - 1] + 1)

            act.dma_start(small[:, :], io["small"]).then_inc(S["loads"], 16)
            act.dma_start(x[:, :], io["x"]).then_inc(S["x_loaded"], 16)
            act.dma_start(ada_b[0:MOD_ROWS, :], io["ada_b"][0]).then_inc(S["adab_landed"], 16)
            act.wait_ge(S["loads"], 16)
            act.activation(cond[:, :], sc("cond", 0, 2 * KD), ACT.Silu).then_inc(S["cond_silu"], 1)
            act.wait_ge(S["cond_silu"], 1)
            act.wait_ge(S["misc_init"], MISC_INIT)
            copy(cond_wide[:, :], gz[:, 0:1].to_broadcast([P, KD * ADA_W]), "cond_zero")
            act.wait_ge(S["cond_zero"], 1)
            copy(cond_wide[:, :].rearrange("p (k n) -> p k n", n=ADA_W)[:, :, 12:14], v3(cond[:, :], 2), "cond_hi")
            for k, name in enumerate(("z_silu", "qk_evac")):
                act.activation(credit[0:1, 4 + k:5 + k], sc("ones", rows=1), ACT.Copy).then_inc(S[name], 2)
            for g in range(ADA_PHASE + 1):
                split_hi(act, g)
            for i in range(DEPTH):
                norm(2 * i)
                if MIXER[i] == "mlstm":
                    mlstm(i)
                else:
                    attention(i)
                norm(2 * i + 1)
                act.wait_ge(S["x_done"], 4 * i + 2)
                if i + 1 == DEPTH:
                    act.dma_start(fw[:, :], io["final_w"]).then_inc(S["fw_landed"], 16)
                else:
                    act.wait_ge(S["modb_done"], 3 * i + 3)
                    act.dma_start(ada_b[0:MOD_ROWS, :], io["ada_b"][i + 1]).then_inc(S["adab_landed"], 16)
                ffn(i)
            squares(2 * DEPTH)
            for s, y in enumerate(("y_prompt", "y_sample")):
                act.wait_ge(S["final_done"], s + 1)
                act.dma_start(io[y][0], xn[:, s * D:(s + 1) * D]).then_inc(S["y_landed"], 16)
            for name, count in (("y_landed", 2), ("c_landed", 16), ("n_landed", 8), ("m_landed", 4), ("kv_landed", 4)):
                act.wait_ge(S[name], 16 * count)

        @block.vector
        def _(dve):
            link = Link(dve, "dve_link")
            row = Link(dve, "row_dve")

            def copy_mod(i, phase, last_tile):
                rows = slice(32 * phase, 32 * phase + 16)
                tile_used(dve, last_tile)
                dve.wait_ge(S["adab_landed"], 16 * (i + 1))
                dve.tensor_tensor(mod_b[rows, :], ADA_PS[0:16, :], ada_b[rows, :], ALU.add).then_inc(S["modb_done"], 1)

            def norm(q):
                if q % 2 == 0:
                    copy_mod(q // 2, 0, INDEX["ada", q // 2, ADA_PHASE - 1])
                dve.wait_ge(S["modT_mm"], q + 1)
                for n, (row, column) in enumerate((SHIFT2, SCALE2) if q % 2 else (SHIFT1, SCALE1)):
                    o = column // P * MOD_ROWS
                    ins = dve.tensor_copy(modT[:, 32 * n:32 * n + 32].rearrange("p (a r) -> p a r", a=2),
                                          v3(MISC[:, o:o + 2 * MOD_ROWS], MOD_ROWS)[:, :, row:row + 16])
                ins.then_inc(S["modT_done"], 1)
                dve.wait_ge(S["modT_done"], q + 1)
                for coef, n in ((coef_b, 0), (coef_a, 1)):
                    for a in range(2):
                        out = coef[:, :].rearrange("p (c a s) -> p a c s", a=2, s=2)[:, a]
                        view = modT[:, 32 * n + 16 * a:32 * n + 16 * a + 16].rearrange("p (g r) -> p g r", r=4)
                        link(dve.tensor_tensor(out, view[:, :, 0:2], view[:, :, 2:4], ALU.add))
                link.wait()
                nw = sc("norm_w", q * KD, KD)
                link(dve.scalar_tensor_tensor(v3(coef_a[:, :], 2), v3(coef_a[:, :], 2), 1.0,
                                              nw.unsqueeze(2).to_broadcast([P, KD, 2]), ALU.add, ALU.mult))
                dve.wait_ge(S["rstd_done"], q + 1)
                for s in range(NS):
                    dve.tensor_scalar(diag[:, s * T:(s + 1) * T], ident, rstd[:, s:s + 1], None,
                                      ALU.mult).then_inc(S["diag_done"], 1)
                link.wait()

                def h_lo(g):
                    dve.wait_ge(S["hhi_done"], 4 * q + g + 1)
                    dve.tensor_tensor(H_lo[:, g * 512:(g + 1) * 512], hf[g % 2][:, :],
                                      H_hi[:, g * 512:(g + 1) * 512].bitcast(F32), ALU.subtract).then_inc(S["h_done"], 1)

                for g in range(4):
                    dve.wait_ge(S["nt_done"], 4 * q + g + 1)
                    if g >= 2:
                        dve.wait_ge(S["h_done"], 4 * q + g - 1)
                    co = slice(4 * g, 4 * g + 4)
                    dve.tensor_tensor(v3(hf[g % 2][:, :], T), v3(ACC[g][:, :], T),
                                      coef_a[:, co].unsqueeze(2).to_broadcast([P, 4, T]),
                                      ALU.mult).then_inc(S["hm_done"], 1)
                    if g:
                        h_lo(g - 1)
                h_lo(3)

            def residual(r, n):
                tile_used(dve, n)
                dve.wait_ge(S["gate_evac"], 4 * r + 4)
                tmp = t1 + ow
                for s in range(NS):
                    for b in (2 * s, 2 * s + 1):
                        link(dve.tensor_tensor(tmp[b][:, :], ACC[b][:, :], gate_bc[:, b * 512:(b + 1) * 512], ALU.mult))
                    link.wait()
                    for b in (2 * s, 2 * s + 1):
                        ins = dve.tensor_tensor(x[:, b * 512:(b + 1) * 512], x[:, b * 512:(b + 1) * 512],
                                                tmp[b][:, :], ALU.add)
                    ins.then_inc(S["x_done"], 1)

            def splits(n0, count):
                if count >= 8:
                    with dve.Fori(0, count // 4) as it:
                        for t in range(4):
                            split_lo(dve, n0 + t + 1, it * 4)
                else:
                    for t in range(count):
                        split_lo(dve, n0 + t + 1)

            def side_taps(dst, bank, blk, it, per, before, after, half_sem, half_base, done_sem):
                views = []
                for b in range(2):
                    o = slice(b * TOK, (b + 1) * TOK)
                    views.append((v3(dst[:, o], T), v3(bank[:, o], T)))
                for b, (d, p) in enumerate(views):
                    dve.scalar_tensor_tensor(d[:, :, 1:T], p[:, :, 0:T - 1], small[:, bass.ds(it * per + before + blk + b, 1)],
                                             d[:, :, 1:T], ALU.mult, ALU.add).then_inc(S[half_sem], 1)
                dve.wait_ge(S[half_sem], half_base)
                for b, (d, p) in enumerate(views):
                    ins = dve.scalar_tensor_tensor(d[:, :, 0:T - 1], p[:, :, 1:T],
                                                   small[:, bass.ds(it * per + after + blk + b, 1)],
                                                   d[:, :, 0:T - 1], ALU.mult, ALU.add)
                ins.then_inc(S[done_sem], 1)

            def part(t, base_, it):
                return t[:, bass.ds(it * 4 * 512 + base_ * 512, 512)]

            def mlstm(i):
                j = ML_INDEX[i]
                n0 = INDEX["ml_x", i, 0]
                w0 = COL["ml_conv_w"] + 3 * j * KI

                def xc_lo(t, it):
                    dve.wait_ge(S["xc_hi"], 8 * j + t + 1 + it * 4)
                    dve.tensor_tensor(part(B_lo, t, it), ow[t % 2][:, :], part(B_hi, t, it).bitcast(F32),
                                      ALU.subtract).then_inc(S["xc_lo"], 1)

                with dve.Fori(0, 2) as it:
                    for t in range(4):
                        k = 8 * j + t
                        split_lo(dve, n0 + t + 1, it * 4)
                        dve.wait_ge(S["xm_hi"], k + 1 + it * 4)
                        dve.wait_ge(S["t1_done"], 2 * k + 2 + it * 8)
                        dve.tensor_tensor(part(A_lo, t, it), UP[t % 2][:, :], part(A_hi, t, it).bitcast(F32),
                                          ALU.subtract)
                        side_taps(t1[t % 2], UP[t % 2], 2 * t, it, 8, w0, w0 + 2 * KI, "conv_half",
                                  2 * k + 2 + it * 8, "conv_done")
                        if t:
                            xc_lo(t - 1, it)
                    xc_lo(3, it)
                dve.wait_ge(S["wg_hi_done"], j + 1)
                dve.tensor_tensor(wg_lo[:, :], wg_raw[:, :], wg_hi[:, :].bitcast(F32),
                                  ALU.subtract).then_inc(S["wg_done"], 1)
                n0 = INDEX["ml_qk", i, 0, 0]
                for g in range(4):
                    split_lo(dve, n0 + 2 * g + 1)
                    if g == 1:
                        dve.wait_ge(S["rows_landed"], 64 * (j + 1))
                        row(dve.scalar_tensor_tensor(gA[0:36, :], gF[0:36, :], -1.0, gF[0:36, :], ALU.mult, ALU.max))
                        row(dve.tensor_scalar(gM[0:36, :], gF[0:36, :], 0.0, None, ALU.min))
                    if g == 2:
                        dve.wait_ge(S["row_act"], ROW_ACT * j + 2)
                        row.wait()
                        row(dve.tensor_tensor(gM[0:36, :], gM[0:36, :], gA[0:36, :], ALU.subtract))
                        row.wait()

                        def scan(dst, src, add, op, initial):
                            for r0, step in ((0, 1), (32, -1)):
                                for s in range(NS):
                                    o = slice(s * T, (s + 1) * T)
                                    rows = slice(r0, r0 + MH)
                                    other = gz[rows, 0:T] if add else src[rows, o][:, ::step]
                                    init = initial(r0, s)
                                    row(dve.tensor_tensor_scan(dst[rows, o][:, ::step], src[rows, o][:, ::step],
                                                               other, init, op, op))
                            row.wait()

                        scan(gb, gM, True, ALU.add, lambda r0, s: 0.0)
                        row(dve.tensor_tensor(gc[0:36, :], gI[0:36, :], gb[0:36, :], ALU.subtract))
                        row.wait()
                        scan(gG, gc, False, ALU.max,
                             lambda r0, s: sc("m0", j, rows=MH, r0=r0) if s else 0.0)
                        row(dve.tensor_scalar(RB[0:36, 0:TOK], gG[0:36, :], -1.0, None, ALU.mult))
                        row(dve.scalar_tensor_tensor(RB[0:36, TOK:2 * TOK], gb[0:36, :], -1.0, gG[0:36, :],
                                                     ALU.mult, ALU.subtract))
                        row.wait()
                        if j:
                            dve.wait_ge(S["m_landed"], 32)
                        for r0, last in ((0, TOK + T - 1), (32, TOK)):
                            dve.tensor_scalar(m_out[r0:r0 + MH, :], RB[r0:r0 + MH, last:last + 1], -1.0, None,
                                              ALU.mult).then_inc(S["m_done"], 1)
                    split_lo(dve, n0 + 2 * g + 2)
                splits(n0 + 8, 8)
                for b in range(4):
                    dve.wait_ge(S["st_mm"], 4 * j + b + 1)
                    dst = (ST, knat)[b // 2]
                    dve.tensor_copy(dst[:, (b % 2) * 512:(b % 2 + 1) * 512], ACC[b][:, :]).then_inc(S["st_evac"], 1)
                dve.wait_ge(S["c_mm"], j + 1)
                row(dve.tensor_copy(ccol[:, :], MISC[:, 0:72]))
                assert row.n == ROW_DVE * (j + 1)
                for half in range(2):
                    n0 = INDEX["ml_v", i, half, 0]
                    splits(n0, 8)
                    tile_used(dve, n0 + 7)
                    for c in range(2):
                        o = DIN + half * 1024 + c * 512
                        dve.tensor_copy(v[:, o:o + 512], ACC[2 + c][:, :]).then_inc(S["v_evac_d"], 1)
                dve.wait_ge(S["xcs_done"], 2 + 8 * (j + 1))
                dve.wait_ge(S["st_evac"], 4 * (j + 1))
                for h in range(MH):
                    head(i, j, h)
                copy_mod(i, 2, INDEX["ada", i, ADA_TILES - 1])
                n0 = INDEX["ml_z", i, 0]

                def z_lo(t, it):
                    dve.wait_ge(S["z_hi"], 8 * j + t + 1 + it * 4)
                    dve.tensor_tensor(part(A_lo, t, it), ow[t % 2][:, :], part(A_hi, t, it).bitcast(F32),
                                      ALU.subtract).then_inc(S["z_lo"], 1)

                dve.wait_ge(S["hc_done"], 4 * (j + 1))
                with dve.Fori(0, 2) as it:
                    for t in range(4):
                        split_lo(dve, n0 + t + 1, it * 4)
                        dve.wait_ge(S["z_lo"], 8 * j + t + 1 + it * 4)
                        dve.wait_ge(S["z_silu"], 2 + 8 * j + t + 1 + it * 4)
                        dve.tensor_tensor(ow[t % 2][:, :], part(XCS, t, it), t1[t % 2][:, :],
                                          ALU.mult).then_inc(S["z_mul"], 1)
                        if t:
                            z_lo(t - 1, it)
                    z_lo(3, it)
                n0 = INDEX["ml_down", i, 0]
                splits(n0, 8)
                residual(2 * i, n0 + 7)

            def head(i, j, h):
                q = 4 * j + h
                n = INDEX["ml_C", i, h]
                dve.wait_ge(S["bc_mm"], q + 1)
                for d, mask in enumerate(("mask_f", "mask_b")):
                    dve.tensor_tensor(v3(E[:, d * TOK:(d + 1) * TOK], T), v3(UP[d][:, 0:TOK], T),
                                      sc(mask, 0, T).unsqueeze(1).to_broadcast([P, NS, T]),
                                      ALU.add).then_inc(S["arg_done"], 1)
                four = lambda ap: ap.rearrange("p (d c t) -> p d c t", d=2, c=2)
                for d in range(2):
                    qv = Q[:, 2 * h * TOK:(2 * h + 2) * TOK].rearrange("p (c s t) -> p c s t", c=2, s=2)[:, :, 1, :]
                    ins = dve.tensor_tensor(four(qs[:, :])[:, d], qv,
                                            ACC[0][:, d * T:(d + 1) * T].unsqueeze(1).to_broadcast([P, 2, T]), ALU.mult)
                ins.then_inc(S["qs_done"], 1)
                split_lo(dve, n - 1)
                dve.wait_ge(S["e_done"], 4 * q + 4)
                for d in range(2):
                    ins = dve.tensor_tensor(Pw[:, d * TOK:(d + 1) * TOK], E[:, d * TOK:(d + 1) * TOK],
                                            ST[:, h * TOK:(h + 1) * TOK], ALU.mult)
                ins.then_inc(S["p_done"], 1)
                split_lo(dve, n)
                dve.wait_ge(S["den_mm"], q + 1)
                dve.wait_ge(S["em_done"], 2 * q + 2)
                link(dve.scalar_tensor_tensor(den[:, :], ACC[1][:, :], -1.0, Em[:, :], ALU.mult, ALU.max))
                link.wait()
                link(dve.tensor_tensor(den[:, :], ACC[1][:, :], den[:, :], ALU.max))
                link.wait()
                link(dve.reciprocal(den[:, :], den[:, :]))
                link.wait()
                for d in range(2):
                    ins = dve.tensor_tensor(four(qs[:, :])[:, d], four(qs[:, :])[:, d],
                                            den[:, d * TOK + T:(d + 1) * TOK].unsqueeze(1).to_broadcast([P, 2, T]),
                                            ALU.mult)
                ins.then_inc(S["qs2_done"], 1)
                link(dve.tensor_tensor(Pw[:, :], Pw[:, :], den[:, :], ALU.mult))
                link.wait()
                dve.tensor_tensor(PT[:, :], Pw[:, 0:TOK], Pw[:, TOK:2 * TOK], ALU.add).then_inc(S["pt_done"], 1)
                dve.wait_ge(S["qs_hi_done"], q + 1)
                dve.tensor_tensor(qs_lo[:, :], qs[:, :], qs_hi[:, :].bitcast(F32),
                                  ALU.subtract).then_inc(S["qs2_done"], 1)
                split_lo(dve, n + 1)
                split_lo(dve, n + 2)
                tile_used(dve, n)
                for s in range(NS):
                    link(dve.bn_stats(bn[:, 6 * s:6 * s + 6], ACC[s][:, :]))
                link.wait()
                for s in range(NS):
                    ins = dve.bn_aggr(mv[:, 2 * s:2 * s + 2], bn[:, 6 * s:6 * s + 6])
                ins.then_inc(S["var_done"], 1)
                dve.wait_ge(S["rstd2_done"], q + 1)
                dve.wait_ge(S["var_done"], q + 1)
                for s in range(NS):
                    dve.tensor_scalar(hn[:, s * DV:(s + 1) * DV], ACC[s][:, :], mv[:, 2 * s:2 * s + 1],
                                      rstd[:, s:s + 1], ALU.subtract, ALU.mult).then_inc(S["hn_done"], 1)
                if h == 1:
                    copy_mod(i, 1, n + 2)
                split_lo(dve, n + 3)
                dve.wait_ge(S["ht_mm"], q + 1)
                for f in range(4):
                    k = 4 * h + f
                    o = slice(k * TOK, (k + 1) * TOK)
                    ins = dve.scalar_tensor_tensor(XCS[:, o], ACC[2 + f // 2][:, (f % 2) * TOK:(f % 2 + 1) * TOK],
                                                   sc("ml_norm_w", j * KI + k), XCS[:, o], ALU.mult, ALU.add)
                ins.then_inc(S["hc_done"], 1)

            def rope(t, c0, heads, own):
                own.wait()
                if c0 != D:
                    dve.wait_ge(S["roped"], 1)
                w = heads * HD
                xv, uv = (ap.rearrange("p (h f e w) -> p h f e w", f=2, e=2, w=16)
                          for ap in (t[:, c0:c0 + w], rope_u[:, 0:w]))
                tab = sc("sin", 0, 64).rearrange("p (f e w) -> p f e w", f=2, e=2)
                for f in range(2):
                    for e in range(2):
                        link(dve.tensor_tensor(uv[:, :, f, e, :], xv[:, :, f, 1 - e, :],
                                               tab[:, f, e, :].unsqueeze(1).to_broadcast([P, heads, 16]), ALU.mult))
                link(dve.tensor_tensor(v3(rope_t[:, 0:w], HD), v3(t[:, c0:c0 + w], HD),
                                       sc("cos", 0, 64).unsqueeze(1).to_broadcast([P, heads, HD]), ALU.mult))
                link.wait()
                dve.tensor_tensor(t[:, c0:c0 + w], rope_t[:, 0:w], rope_u[:, 0:w], ALU.add).then_inc(S["roped"], 1)

            def attention(i):
                a = i - 1
                if a == 0:
                    n0 = INDEX["q", i, 0]
                    splits(n0, 4)
                    tile_used(dve, n0 + 3)
                    rows_q = Link(dve, "row_q_d")
                    for c in range(2):
                        rows_q(dve.tensor_copy(qrow[:, D + c * 512:D + (c + 1) * 512], ACC[2 + c][:, :]))
                    n0 = INDEX["kv", i, 0]
                    splits(n0, 1)
                    rope(qrow, D, NH, rows_q)
                    splits(n0 + 1, 1)
                    tile_used(dve, n0 + 1)
                    rows_k = Link(dve, "row_k")
                    for s in range(NS):
                        rows_k(dve.tensor_copy(
                            krow[:, s * 512:(s + 1) * 512].rearrange("p (h e d) -> p h e d", e=2, d=HD),
                            UP[s][:, 0:256].rearrange("p (h e d) -> p h e d", e=1, d=HD)
                            .to_broadcast([P, KV, 2, HD])))
                    rope(krow, 512, 2 * KV, rows_k)
                    link(dve.tensor_scalar(nsink[:, :], sc("sink", 0, NH), -1.0, None, ALU.mult))
                else:
                    for c, rows in enumerate((qrow, krow, vrow)):
                        n0 = INDEX["qkv", i, c, 0]
                        splits(n0, 4)
                        tile_used(dve, n0 + 3)
                        for k in range(2):
                            dve.tensor_copy(rows[:, D + k * 512:D + (k + 1) * 512], ACC[2 + k][:, :]
                                            ).then_inc(S["row_q_d"], 1)
                    dve.wait_ge(S["bias_landed"], 16)
                    link(dve.tensor_tensor(v3(bias[:, :], T), v3(bias[:, :], T),
                                           sc("na_mask", 0, T).unsqueeze(1).to_broadcast([P, NH, T]), ALU.add))
                for b in range(4):
                    dve.wait_ge(S["tq_mm"], 4 * a + b + 1)
                    dve.tensor_copy(qT[:, b * 512:(b + 1) * 512], ACC[b][:, :]).then_inc(S["tq_evac"], 1)
                n = INDEX["ada", i, ADA_PHASE]

                def maxima(u):
                    g, s = u // 2, u % 2
                    w = 8 * a + u
                    width = (1 + s) * T
                    dve.wait_ge(S["s_mm"], w + 1)
                    if s == 0 or a == 0:
                        for b in range(2):
                            link(dve.tensor_reduce(mx[:, 2 * b:2 * b + 2], v3(SCORES[s][b][:, 0:2 * width], width),
                                                   AX_X, ALU.max))
                    else:
                        for b in range(2):
                            sa, sp_ = v3(Sa[:, b * 512:(b + 1) * 512], TOK), v3(SCORES[s][b][:, :], TOK)
                            hd = 4 * g + 2 * b
                            link(dve.scalar_tensor_tensor(sa[:, :, 0:T], sp_[:, :, 0:T], HD ** -0.5,
                                                          v3(bias[:, hd * T:(hd + 2) * T], T), ALU.mult, ALU.add))
                            link(dve.tensor_scalar(sa[:, :, T:TOK], sp_[:, :, T:TOK], HD ** -0.5, None, ALU.mult))
                        link.wait()
                        link(dve.tensor_reduce(mx[:, :], v3(Sa[:, :], TOK), AX_X, ALU.max))
                    link.wait()
                    if a == 0:
                        dve.scalar_tensor_tensor(nm[:, :], mx[:, :], -HD ** -0.5, nsink[:, 4 * g:4 * g + 4], ALU.mult,
                                                 ALU.min).then_inc(S["nm_done"], 1)
                        dve.wait_ge(S["nm_done"], w + 1)
                        dve.tensor_tensor(esink[:, :], nm[:, :], nsink[:, 4 * g:4 * g + 4],
                                          ALU.subtract).then_inc(S["esink_in"], 1)
                    else:
                        dve.tensor_scalar(nm[:, :], mx[:, :], -1.0 if s else -HD ** -0.5, None,
                                          ALU.mult).then_inc(S["nm_done"], 1)

                maxima(0)
                for u in range(8):
                    g, s = u // 2, u % 2
                    w = 8 * a + u
                    width = (1 + s) * T
                    dve.wait_ge(S["exp_done"], 4 * w + 4)
                    if a == 0:
                        dve.wait_ge(S["esink_done"], w + 1)
                        link(dve.tensor_tensor(sums[:, :], sums[:, :], esink[:, :], ALU.add))
                        link.wait()
                    if w:
                        dve.wait_ge(S["pn_done"], w)
                    dve.reciprocal(rsum[:, :], sums[:, :]).then_inc(S["rsum_done"], 1)
                    if u < 7:
                        maxima(u + 1)
                    split_lo(dve, n + 2 * u + 1)
                    split_lo(dve, n + 2 * u + 2)
                    if u == 3:
                        copy_mod(i, 1, n + 2 * u + 1)
                    dve.wait_ge(S["o_hi"], 2 * w + 2)
                    for e in range(2):
                        dve.tensor_tensor(out_half(H_lo, g, s, e), psum_half(e), out_half(H_hi, g, s, e).bitcast(F32),
                                          ALU.subtract).then_inc(S["o_lo"], 1)
                copy_mod(i, 2, INDEX["ada", i, ADA_TILES - 1])
                n0 = INDEX["o", i, 0]
                splits(n0, 4)
                residual(2 * i, n0 + 3)

            def ffn(i):
                n0 = INDEX["ffn_up", i, 0]
                w0 = COL["ffn_conv_w"] + 3 * i * FB

                def step(j, n, adv=0, jj=0, with_ada=False):
                    k = NJ * i + j
                    split_lo(dve, n + 1, adv)
                    dve.wait_ge(S["tg_done"], 2 * k + 2 + jj * 2)
                    side_taps(tg, UP[0], 2 * j, jj, 2, w0, w0 + 2 * FB, "cg_half", 2 * k + 2 + jj * 2, "cg_done")
                    split_lo(dve, n + 2, adv)
                    dve.wait_ge(S["tv_done"], 2 * k + 2 + jj * 2)
                    side_taps(tv, UP[1], FB // 2 + 2 * j, jj, 2, w0, w0 + 2 * FB, "cv_half", 2 * k + 2 + jj * 2,
                              "cv_done")
                    if j > 0:
                        split_lo(dve, n + 3, adv)
                    if with_ada:
                        split_lo(dve, n + 4, adv)
                    dve.wait_ge(S["ghi_done"], k + 1 + jj)
                    dve.tensor_tensor(G_lo[:, :], gt[:, :], G_hi[:, :].bitcast(F32),
                                      ALU.subtract).then_inc(S["glo_done"], 1)

                per = 4 if i + 1 < DEPTH else 3
                step(0, n0)
                step(1, n0 + 2)
                with dve.Fori(0, 2) as it:
                    for r in range(4):
                        step(2 + r, n0 + 5 + per * r, it * (4 * per), it * 4, per == 4)
                step(10, n0 + 5 + 8 * per)
                split_lo(dve, INDEX["ffn_down", i, NJ - 1] + 1)
                residual(2 * i + 1, INDEX["ffn_down", i, NJ - 1])

            for k, name in enumerate(("conv_done", "xc_lo", "z_mul", "z_lo")):
                dve.memset(credit[0:1, k:k + 1], 0.0).then_inc(S[name], 2)
            dve.wait_ge(S["misc_init"], MISC_INIT)
            dve.wait_ge(S["cond_hi"], 1)
            wide = cond_wide[:, :].rearrange("p (k n) -> p k n", n=ADA_W)
            dve.tensor_tensor(wide[:, :, 14:16], v3(cond[:, :], 2), wide[:, :, 12:14].bitcast(F32),
                              ALU.subtract).then_inc(S["cond_lo"], 1)
            for g in range(ADA_PHASE + 1):
                split_lo(dve, g)
            for i in range(DEPTH):
                norm(2 * i)
                if MIXER[i] == "mlstm":
                    mlstm(i)
                else:
                    attention(i)
                norm(2 * i + 1)
                ffn(i)
            dve.wait_ge(S["rstd_done"], 2 * DEPTH + 1)
            dve.wait_ge(S["fw_landed"], 16)
            for s in range(NS):
                o = slice(s * D, (s + 1) * D)
                dve.scalar_tensor_tensor(xn[:, o], x[:, o], rstd[:, s:s + 1], fw[:, :], ALU.mult,
                                         ALU.mult).then_inc(S["final_done"], 1)

        @block.gpsimd
        def _(pool):
            chain = Link(pool, "pool_chain")
            zeroed = [gI, gF, gA, gM, gb, gc, gG, RB, RBW, gz, mod_b]
            for t in zeroed:
                pool.memset(t[:, :], 0.0).then_inc(S["misc_init"], 1)
            pool.memset(half_pow[:, :], -0.5).then_inc(S["misc_init"], 1)
            assert len(zeroed) + 1 == MISC_INIT
            pool.memset(credit[0:1, 6:7], 0.0).then_inc(S["xcs_done"], 2)
            pool.wait_ge(S["misc_init"], MISC_INIT)
            pool.wait_ge(S["loads"], 16)

            def inverse_root(src, scale, done):
                if chain.n:
                    chain.wait()
                chain(pool.tensor_scalar(var[:, :], src, scale, EPS, ALU.mult, ALU.add))
                chain.wait()
                pool.tensor_tensor(rstd[:, :], var[:, :], half_pow[:, :], ALU.pow).then_inc(S[done], 1)

            def norm(q, shift=True):
                pool.wait_ge(S["ssq_done"], 2 * q + 2)
                inverse_root(ssq[:, :], 1.0 / D, "rstd_done")
                for g in range(4 if shift else 0):
                    pool.wait_ge(S["hm_done"], 4 * q + g + 1)
                    t = v3(hf[g % 2][:, :], T)
                    pool.tensor_tensor(t, t, coef_b[:, 4 * g:4 * g + 4].unsqueeze(2).to_broadcast([P, 4, T]),
                                       ALU.add).then_inc(S["hf_done"], 1)

            for i in range(DEPTH):
                norm(2 * i)
                if MIXER[i] == "mlstm":
                    j = ML_INDEX[i]
                    with pool.Fori(0, 2) as it:
                        for t in range(4):
                            pool.wait_ge(S["xc_done"], 8 * j + t + 1 + it * 4)
                            skip = small[:, bass.ds(it * 8 + COL["ml_skip"] + j * KI + 2 * t, 2)]
                            pool.tensor_tensor(v3(XCS[:, bass.ds(it * 2048 + t * 512, 512)], TOK), v3(ow[t % 2][:, :], TOK),
                                               skip.unsqueeze(2).to_broadcast([P, 2, TOK]),
                                               ALU.mult).then_inc(S["xcs_done"], 1)
                    for h in range(MH):
                        q = 4 * j + h
                        pool.wait_ge(S["var_done"], q + 1)
                        if q:
                            pool.wait_ge(S["hn_done"], 2 * q)
                        inverse_root(v3(mv[:, :], 2)[:, :, 1], 1.0, "rstd2_done")
                else:
                    for u in range(8):
                        width = (1 + u % 2) * T
                        pool.wait_ge(S["rsum_done"], 8 * (i - 1) + u + 1)
                        ev = v3(Ea[u % 2][:, 0:4 * width], width)
                        pool.tensor_tensor(ev, ev, rsum[:, :].unsqueeze(2).to_broadcast([P, 4, width]),
                                           ALU.mult).then_inc(S["pn_done"], 1)
                norm(2 * i + 1)

                def gated(k, kk):
                    pool.wait_ge(S["sg_done"], k + 1 + kk)
                    pool.wait_ge(S["cv_done"], k + 1 + kk)
                    if k:
                        pool.wait_ge(S["glo_done"], k + kk)
                    pool.tensor_tensor(gt[:, :], sg[:, :], tv[:, :], ALU.mult).then_inc(S["gt_done"], 1)

                gated(NJ * i, 0)
                with pool.Fori(0, NJ - 1) as it:
                    gated(NJ * i + 1, it)
            norm(2 * DEPTH, shift=False)


ROW_ABS, ROW_C, ROW_G, ROW_DVE = 1, 8, 13, 15
ROW_ACT = 3
MISC_INIT = 12


def kernel(**inputs):
    import concourse.bacc as bacc
    from concourse.bass_utils import run_bass_kernel_spmd

    nc = bacc.Bacc("TRN2", target_bir_lowering=False, num_devices=1, dynamic_dma_scratch_size=1024)
    arrays = {f"in_{k}": np.ascontiguousarray(a) for k, a in
              host_arrays({k: np.asarray(a) for k, a in inputs.items()}).items()}
    io = {}
    for k, a in arrays.items():
        io[k[3:]] = nc.dram_tensor(k, a.shape, F32, kind="ExternalInput").ap()
    for name, shape in OUTPUTS:
        io[name] = nc.dram_tensor(f"out_{name}", shape, F32, kind="ExternalOutput").ap()
    build(nc, io)
    r = run_bass_kernel_spmd(nc, [arrays], core_ids=[0])
    return tuple(r.results[0][f"out_{name}"] for name, _ in OUTPUTS)
```
